# Optimizing a Trainium2 kernel written in Bass

```python
import jax, jax.numpy as jnp
from jax import lax
import numpy as np

D_MODEL = 1024
BATCH = 1
SEQ = 512
DEPTH = 2
DEC_BATCH = 1
DEC_SEQ = 64
PAST_LEN = 256

CHUNK = 64
N_META = 16
Q_BLOCK = 128
N_A_LAYERS = DEPTH // 2
N_B_LAYERS = DEPTH - N_A_LAYERS
FOX_HEAD_DIM = 64
FOX_HEADS = D_MODEL // FOX_HEAD_DIM
FOX_WIDTH = FOX_HEADS * FOX_HEAD_DIM
MLA_HEADS = 16
MLA_NOPE = 64
MLA_ROPE = 32
MLA_V = 64
KV_RANK = D_MODEL // 4
Q_RANK = 3 * D_MODEL // 8
D_FF = 4 * D_MODEL
ROPE_BASE = 10000.0
RMS_EPS = 1e-6
NEG = -1e30
FOX_SCALE = FOX_HEAD_DIM ** -0.5
MLA_SCALE = (MLA_NOPE + MLA_ROPE) ** -0.5

kernel_name = 'yoco_fox_mla_streaming_encoder_step'

def rmsnorm(x, g):
    xf = x.astype(jnp.float32)
    y = xf * lax.rsqrt(jnp.mean(xf * xf, axis=-1, keepdims=True) + RMS_EPS)
    return (y * g.astype(jnp.float32)).astype(x.dtype)

def sq_relu_mlp(h, w_up, w_down):
    return jnp.square(jax.nn.relu(h @ w_up)) @ w_down

def rope(x, pos):
    r = x.shape[-1]
    half = r // 2
    inv = 1.0 / (ROPE_BASE ** (jnp.arange(half, dtype=jnp.float32) * (2.0 / r)))
    ang = pos.astype(jnp.float32)[:, None] * inv[None, :]
    shape = (1, pos.shape[0]) + (1,) * (x.ndim - 3) + (half,)
    cos = jnp.cos(ang).reshape(shape)
    sin = jnp.sin(ang).reshape(shape)
    xf = x.astype(jnp.float32)
    x1, x2 = xf[..., :half], xf[..., half:]
    return jnp.concatenate([x1 * cos - x2 * sin, x2 * cos + x1 * sin], axis=-1).astype(x.dtype)

def fox_project(h, w_in, b_f):
    bsz, t, _ = h.shape
    z = h @ w_in
    qkv = z[..., :3 * FOX_WIDTH].reshape(bsz, t, 3, FOX_HEADS, FOX_HEAD_DIM)
    logf = jax.nn.log_sigmoid((z[..., 3 * FOX_WIDTH:] + b_f).astype(jnp.float32))
    return qkv[:, :, 0], qkv[:, :, 1], qkv[:, :, 2], logf

def fox_block(q, k, v, f_q, f_k, mask):
    logits = jnp.einsum('bqhd,bkhd->bhqk', q, k).astype(jnp.float32) * FOX_SCALE
    decay = jnp.transpose(f_q, (0, 2, 1))[..., :, None] - jnp.transpose(f_k, (0, 2, 1))[..., None, :]
    logits = jnp.where(mask, logits + decay, NEG)
    p = jax.nn.softmax(logits, axis=-1).astype(v.dtype)
    return jnp.einsum('bhqk,bkhd->bqhd', p, v)

def fox_attention_prompt(q, k, v, logf):
    tp = q.shape[1]
    cum = jnp.cumsum(logf, axis=1)
    pos = jnp.arange(tp)
    outs = []
    for s in range(0, tp, Q_BLOCK):
        e = s + Q_BLOCK
        mask = pos[s:e, None] >= pos[None, :e]
        outs.append(fox_block(q[:, s:e], k[:, :e], v[:, :e], cum[:, s:e], cum[:, :e], mask))
    return jnp.concatenate(outs, axis=1)

def fox_attention_step(q, k_all, v_all, logf_all):
    s_len = q.shape[1]
    k_len = k_all.shape[1]
    past = k_len - s_len
    cum = jnp.cumsum(logf_all.astype(jnp.float32), axis=1)
    mask = jnp.arange(k_len)[None, :] <= past + jnp.arange(s_len)[:, None]
    return fox_block(q, k_all, v_all, cum[:, past:], cum, mask)

def mla_shared_latent(x, kv_norm, w_kv_down, ckv_norm, pos):
    z = rmsnorm(x, kv_norm) @ w_kv_down
    ckv = rmsnorm(z[..., :KV_RANK], ckv_norm)
    krope = rope(z[..., KV_RANK:], pos)
    return ckv, krope

def mla_decompress(ckv, w_kv_up):
    bsz, t, _ = ckv.shape
    kv = (ckv @ w_kv_up).reshape(bsz, t, MLA_HEADS, MLA_NOPE + MLA_V)
    return kv[..., :MLA_NOPE], kv[..., MLA_NOPE:]

def mla_queries(h, w_q_down, q_norm, w_q_up, pos):
    bsz, t, _ = h.shape
    cq = rmsnorm(h @ w_q_down, q_norm)
    q = (cq @ w_q_up).reshape(bsz, t, MLA_HEADS, MLA_NOPE + MLA_ROPE)
    return q[..., :MLA_NOPE], rope(q[..., MLA_NOPE:], pos)

def mla_block(q_nope, q_rope, k_nope, k_rope, v, mask):
    logits = (jnp.einsum('bqhn,bkhn->bhqk', q_nope, k_nope)
              + jnp.einsum('bqhr,bkr->bhqk', q_rope, k_rope)).astype(jnp.float32) * MLA_SCALE
    if mask is not None:
        logits = jnp.where(mask, logits, NEG)
    p = jax.nn.softmax(logits, axis=-1).astype(v.dtype)
    return jnp.einsum('bhqk,bkhv->bqhv', p, v)

def mla_attention_prompt(q_nope, q_rope, k_nope, k_rope, v, cid):
    tp = q_nope.shape[1]
    outs = []
    for s in range(0, tp, Q_BLOCK):
        e = s + Q_BLOCK
        kl = min(tp, e + CHUNK)
        mask = cid[s:e, None] >= cid[None, :kl]
        outs.append(mla_block(q_nope[:, s:e], q_rope[:, s:e], k_nope[:, :kl],
                              k_rope[:, :kl], v[:, :kl], mask))
    return jnp.concatenate(outs, axis=1)

def trunk(x, pos, n_valid, cid, past, params):
    (norm_mix, norm_ffn, w_in_a, b_f, w_o_a, kv_norm, w_kv_down, ckv_norm, w_kv_up,
     w_q_down, q_norm, w_q_up, w_o_b, w_up, w_down, final_norm) = params
    bsz, t = x.shape[0], x.shape[1]
    fox_k, fox_v, fox_f = [], [], []
    for l in range(DEPTH):
        h = rmsnorm(x, norm_mix[l])
        if l < N_A_LAYERS:
            q, k, v, logf = fox_project(h, w_in_a[l], b_f[l])
            fox_k.append(k[:, :n_valid])
            fox_v.append(v[:, :n_valid])
            fox_f.append(logf[:, :n_valid])
            if past is None:
                o = fox_attention_prompt(q, k, v, logf)
            else:
                o = fox_attention_step(q,
                                       jnp.concatenate([past[0][l], k], axis=1),
                                       jnp.concatenate([past[1][l], v], axis=1),
                                       jnp.concatenate([past[2][l], logf], axis=1))
            x = x + o.reshape(bsz, t, FOX_WIDTH) @ w_o_a[l]
        else:
            b = l - N_A_LAYERS
            if b == 0:
                ckv, krope = mla_shared_latent(x, kv_norm, w_kv_down, ckv_norm, pos)
                new_ckv, new_krope = ckv[:, :n_valid], krope[:, :n_valid]
                if past is not None:
                    ckv = jnp.concatenate([past[3], ckv], axis=1)
                    krope = jnp.concatenate([past[4], krope], axis=1)
                k_nope, v_mla = mla_decompress(ckv, w_kv_up)
            q_nope, q_rope = mla_queries(h, w_q_down[b], q_norm[b], w_q_up[b], pos)
            if past is None:
                o = mla_attention_prompt(q_nope, q_rope, k_nope, krope, v_mla, cid)
            else:
                o = mla_block(q_nope, q_rope, k_nope, krope, v_mla, None)
            x = x + o.reshape(bsz, t, MLA_HEADS * MLA_V) @ w_o_b[b]
        x = x + sq_relu_mlp(rmsnorm(x, norm_ffn[l]), w_up[l], w_down[l])
    y = rmsnorm(x, final_norm)
    return y, jnp.stack(fox_k), jnp.stack(fox_v), jnp.stack(fox_f), new_ckv, new_krope

def setup_inputs(seed: int = 0) -> dict:
    key = jax.random.key(seed)
    ks = jax.random.split(key, 32)
    f32 = jnp.float32

    def nrm(k, shape, scale=1.0):
        return jax.random.normal(k, shape, f32) * scale

    return {
        'x_prompt': nrm(ks[0], (BATCH, SEQ, D_MODEL)),
        'x_sample': nrm(ks[1], (DEC_BATCH, DEC_SEQ, D_MODEL)),
        'cache_fox_k': nrm(ks[2], (N_A_LAYERS, DEC_BATCH, PAST_LEN, FOX_HEADS, FOX_HEAD_DIM)),
        'cache_fox_v': nrm(ks[3], (N_A_LAYERS, DEC_BATCH, PAST_LEN, FOX_HEADS, FOX_HEAD_DIM)),
        'cache_fox_logf': jax.nn.log_sigmoid(4.5 + nrm(ks[4], (N_A_LAYERS, DEC_BATCH, PAST_LEN, FOX_HEADS), 1.5)),
        'cache_mla_ckv': nrm(ks[5], (DEC_BATCH, PAST_LEN, KV_RANK)),
        'cache_mla_krope': nrm(ks[6], (DEC_BATCH, PAST_LEN, MLA_ROPE)),
        'meta_tokens': nrm(ks[7], (N_META, D_MODEL)),
        'norm_mix': 1.0 + nrm(ks[8], (DEPTH, D_MODEL), 0.02),
        'norm_ffn': 1.0 + nrm(ks[9], (DEPTH, D_MODEL), 0.02),
        'w_in_a': nrm(ks[10], (N_A_LAYERS, D_MODEL, 3 * FOX_WIDTH + FOX_HEADS), D_MODEL ** -0.5),
        'b_f': 3.0 + 3.0 * jax.random.uniform(ks[11], (N_A_LAYERS, FOX_HEADS), f32),
        'w_o_a': nrm(ks[12], (N_A_LAYERS, FOX_WIDTH, D_MODEL), FOX_WIDTH ** -0.5),
        'kv_norm': 1.0 + nrm(ks[13], (D_MODEL,), 0.02),
        'w_kv_down': nrm(ks[14], (D_MODEL, KV_RANK + MLA_ROPE), D_MODEL ** -0.5),
        'ckv_norm': 1.0 + nrm(ks[15], (KV_RANK,), 0.02),
        'w_kv_up': nrm(ks[16], (KV_RANK, MLA_HEADS * (MLA_NOPE + MLA_V)), KV_RANK ** -0.5),
        'w_q_down': nrm(ks[17], (N_B_LAYERS, D_MODEL, Q_RANK), D_MODEL ** -0.5),
        'q_norm': 1.0 + nrm(ks[18], (N_B_LAYERS, Q_RANK), 0.02),
        'w_q_up': nrm(ks[19], (N_B_LAYERS, Q_RANK, MLA_HEADS * (MLA_NOPE + MLA_ROPE)), Q_RANK ** -0.5),
        'w_o_b': nrm(ks[20], (N_B_LAYERS, MLA_HEADS * MLA_V, D_MODEL), (MLA_HEADS * MLA_V) ** -0.5),
        'w_up': nrm(ks[21], (DEPTH, D_MODEL, D_FF), D_MODEL ** -0.5),
        'w_down': nrm(ks[22], (DEPTH, D_FF, D_MODEL), D_FF ** -0.5),
        'final_norm': 1.0 + nrm(ks[23], (D_MODEL,), 0.02),
    }

def reference(x_prompt, x_sample, cache_fox_k, cache_fox_v, cache_fox_logf, cache_mla_ckv,
              cache_mla_krope, meta_tokens, norm_mix, norm_ffn, w_in_a, b_f, w_o_a, kv_norm,
              w_kv_down, ckv_norm, w_kv_up, w_q_down, q_norm, w_q_up, w_o_b, w_up, w_down,
              final_norm):
    params = (norm_mix, norm_ffn, w_in_a, b_f, w_o_a, kv_norm, w_kv_down, ckv_norm, w_kv_up,
              w_q_down, q_norm, w_q_up, w_o_b, w_up, w_down, final_norm)

    bsz = x_prompt.shape[0]
    meta = jnp.broadcast_to(meta_tokens.astype(x_prompt.dtype)[None], (bsz, N_META, x_prompt.shape[2]))
    xp = jnp.concatenate([meta, x_prompt], axis=1)
    t = xp.shape[1]
    tp = -(-t // Q_BLOCK) * Q_BLOCK
    xp = jnp.pad(xp, ((0, 0), (0, tp - t), (0, 0)))
    pos_p = jnp.arange(tp)
    cid = jnp.where(pos_p < N_META, -1, (pos_p - N_META) // CHUNK)
    cid = jnp.where(pos_p < t, cid, tp)
    yp, pk, pv, pf, pc, pr = trunk(xp, pos_p, t, cid, None, params)
    y_prompt = yp[:, N_META:t]

    past_len = cache_mla_ckv.shape[1]
    s_len = x_sample.shape[1]
    pos_s = past_len + jnp.arange(s_len)
    past = (cache_fox_k, cache_fox_v, cache_fox_logf, cache_mla_ckv, cache_mla_krope)
    y_sample, sk, sv, sf, sc, sr = trunk(x_sample, pos_s, s_len, None, past, params)

    return (y_prompt, y_sample, pk, pv, pf, pc, pr, sk, sv, sf, sc, sr)


_drawn_inputs = setup_inputs


def setup_inputs(seed=0):
    import zlib

    import numpy as np

    out = dict(_drawn_inputs(seed))
    spreads = {}
    factors = {'norm_mix': 2.867,
     'kv_norm': 2.77,
     'ckv_norm': 3.042,
     'q_norm': 8.0,
     'final_norm': 8.418,
     'cache_mla_ckv': 2.791,
     'cache_mla_krope': 4.05}
    for name, (base, spread) in spreads.items():
        noise = np.random.default_rng([zlib.crc32(name.encode()), seed]).standard_normal(out[name].shape)
        drawn = base * np.exp(spread * noise) if base else spread * noise
        out[name] = __import__('jax').numpy.asarray(drawn.astype(out[name].dtype))
    for name, factor in factors.items():
        out[name] = (out[name] * factor).astype(out[name].dtype)
    return out
```

```python
from contextlib import ExitStack

import concourse.bass as bass
from concourse import mybir

F32 = mybir.dt.float32
F32R = mybir.dt.float32r
ALU = mybir.AluOpType
ACT = mybir.ActivationFunctionType
AX = mybir.AxisListType

P = 128
D = 1024
KD = D // P
SEQ, SAM, META, PAST = 512, 64, 16, 256
T = SEQ + SAM + META
TX = SAM + META
NT = SEQ // P
TH = T // 2
T1 = SEQ + SAM
KEYS = T + PAST
HEADS, HD = 16, 64
PAIRS = HEADS // 2
ROPE = 32
KVR, QR = D // 4, 3 * D // 8
DFF = 4 * D
CH = 256
NCH = DFF // CH
EPS = 1e-6
FOX_SCALE = HD ** -0.5
MLA_SCALE = (HD + ROPE) ** -0.5
HALF = 2048
R_FOX, R_MLA = HD + 2, HD + ROPE
TILE_ROWS = [P] * NT + [TX]

W_IN0, WO_A0, MLP_A0 = 0, 12, 16
KVD0, QD0, KVU0, QU0, WO_B0, MLP_B0, W_END = 48, 50, 52, 54, 58, 62, 94

C_ID, C_U, C_ONE, C_META, C_TRI, C_SAM, C_COS, C_SIN = 0, 128, 256, 384, 512, 592, 672, 752
C_N = 832
M_N = 2 * (P + META + SAM + PAST)
MD = P + META + SAM + PAST


def unit_keys(u):
    return (PAST + SAM, META + P * (u + 1)) if u < NT else (0, PAST + SAM + META)


ACC_N = KD * (NCH + 1)
F_CHAIN = 18
P_OFF = [0, 208, 544, 1008, 1600]
P_N = 1984


def build(nc, io):
    ctx = ExitStack()
    with ctx:
        base = 16512
        top = {"at": base}

        def region(nbytes):
            at = top["at"]
            top["at"] = at + (nbytes + 31) // 32 * 32
            assert top["at"] <= nc.sbuf_usable_end, top["at"]
            return at

        def at(name, shape, dt, offset):
            return nc.alloc_sbuf_tensor_at(name, shape, dt, offset=(offset + 31) // 32 * 32)

        def sb(name, shape, dt=F32):
            n = 4
            for s in shape[1:]:
                n *= s
            return at(name, shape, dt, region(n))

        R_RAW = region(4 * HALF * 4)
        R_W = region(8 * HALF * 4)
        R_G = region(2 * KD * T * 4)
        R_O = region(2 * KD * T * 4)
        raw = at("raw", [P, 4, HALF], F32, R_RAW)
        wh = at("wh", [P, 4, HALF], F32R, R_W)
        wl = at("wl", [P, 4, HALF], F32R, R_W + 4 * HALF * 4)
        xT = sb("xT", [P, KD, T])
        o = R_W
        pth = at("pth", [P, 2800], F32R, o); o += 11200
        ptl = at("ptl", [P, 2800], F32R, o); o += 11200
        qh = at("qh", [R_MLA, 2, T], F32R, o); o += 8 * T
        ql = at("ql", [R_MLA, 2, T], F32R, o); o += 8 * T
        kh = at("kh", [R_MLA, 2, KEYS], F32R, o); o += 8 * KEYS
        kl = at("kl", [R_MLA, 2, KEYS], F32R, o); o += 8 * KEYS
        prob = at("prob", [P, 2, P_N], F32, (o + 31) // 32 * 32)
        xgh = at("xgh", [P, KD, T], F32R, R_G)
        xgl = at("xgl", [P, KD, T], F32R, R_G + KD * T * 4)
        natq = [at("natq0", [P, 5, 2 * R_FOX], F32, R_G), at("natq1", [P, 5, 2 * R_MLA], F32, R_G)]
        natk = [at("natk0", [P, 7, 2 * R_FOX], F32, R_G + 2656),
                at("natk1", [P, 7, 4 * HD], F32, R_G + 3840)]
        natv0 = at("natv0", [P, 7, P], F32, R_G + 2656 + 3712)
        vh = at("vh", [P, 7, P], F32R, R_G + 11008)
        vl = at("vl", [P, 7, P], F32R, R_G + 11008 + 3584)
        yT = at("yT", [P, KD, T1], F32, R_G)
        oh = at("oh", [P, PAIRS, T], F32R, R_O)
        ol = at("ol", [P, PAIRS, T], F32R, R_O + KD * T * 4)
        xn = at("xn", [P, 5, D], F32, R_O)
        ckn = at("ckn", [P, 2, D], F32, R_O + 20480)
        cka = at("cka", [P, 2, HEADS, R_FOX], F32, R_O + 28672)
        stg = at("stg", [P, 4, 8 * R_FOX], F32, R_O)
        acc = at("acc", [P, KD, T], F32, R_O)
        hh = at("hh", [P, 2, 2, T], F32R, R_O + 18944)
        hl = at("hl", [P, 2, 2, T], F32R, R_O + 18944 + 9472)
        ckvTh = at("ckvTh", [P, 2, KEYS], F32R, R_O)
        ckvTl = at("ckvTl", [P, 2, KEYS], F32R, R_O + 6784)
        cqTh = at("cqTh", [P, 3, T], F32R, R_O + 13568)
        cqTl = at("cqTl", [P, 3, T], F32R, R_O + 13568 + 7104)
        zc = at("zc", [P, 7, KVR], F32, R_O + 13568)
        zq = at("zq", [P, 5, QR], F32, R_O + 27776)
        gckv = at("gckv", [P, KVR], F32, R_O + 35456)
        stn = at("stn", [P, 4, 512], F32, R_G)
        rtmp = at("rtmp", [P, 4, 4, ROPE // 2], F32, R_G + 8192)
        yst = at("yst", [P, 2, D], F32, R_O)
        mraw = at("mraw", [P, M_N], F32, R_RAW)

        cst = sb("cst", [P, C_N])
        idr = sb("idr", [P, P], F32R)
        mask = sb("mask", [P, M_N], F32R)
        gn = at("gn", [48, P], F32, R_RAW + HALF * 4)
        gT = sb("gT", [P, 48])
        bfb = sb("bfb", [P, HEADS])
        gq = at("gq", [P, QR], F32, R_G + 24000)
        sq = sb("sq", [P, 2, T])
        sacc = sb("sacc", [P, 5 * P])
        small = region(4 * T)
        r2T = at("r2T", [P, T], F32, small)
        v5 = sb("v5", [P, 5])
        rst = sb("rst", [P, 5])
        rst8 = sb("rst8", [P, 5])
        ss = sb("ss", [P, 2, 5])
        rc = sb("rc", [P, 2, 5])
        mhalf = sb("mhalf", [P, 5])
        wf = at("wf", [P, KD, HEADS], F32, small)
        wfh = at("wfh", [P, KD, HEADS], F32R, small + 512)
        wfl = at("wfl", [P, KD, HEADS], F32R, small + 1024)
        lg = sb("lg", [P, 7, HEADS])
        FQ = at("FQ", [P, 5, HEADS, 2], F32, small + 1536)
        keys = region(4 * 7 * HEADS * 2)
        FK = at("FK", [P, 7, HEADS, 2], F32, keys)
        nmx = sb("nmx", [P, 5])
        sm = sb("sm", [P, 5])
        rs = sb("rs", [P, 5])
        krn = at("krn", [P, 7, ROPE], F32, R_G + 20000)
        zr = at("zr", [P, 5, ROPE], F32, keys)
        krt = at("krt", [P, 4, 5, ROPE // 2], F32, R_G + 21056)
        ft = sq[:, 0, 0:480].rearrange("p (a b) -> p a b", a=6)
        ident = cst[:, C_ID:C_ID + P]
        ones = cst[:, C_ONE:C_ONE + P]

        qscr = [nc.dram_tensor("q_fox", (T, HEADS * R_FOX), F32, kind="Internal").ap(),
                nc.dram_tensor("q_mla", (T, HEADS * R_MLA), F32, kind="Internal").ap()]
        kscr = [nc.dram_tensor("k_fox", (KEYS, HEADS * R_FOX), F32, kind="Internal").ap(),
                nc.dram_tensor("kv_mla", (KEYS, HEADS * 2 * HD), F32, kind="Internal").ap()]

        ps = ctx.enter_context(nc.psum_tensor("ps", [P, 8, 512], F32))
        pf = ps[:, :, :].rearrange("p b c -> p (b c)")

        def sem(name):
            return ctx.enter_context(nc.semaphore(name))

        cst_in, mask_in, x_in, small_in = sem("cst_in"), sem("mask_in"), sem("x_in"), sem("small_in")
        gain_in = sem("gain_in")
        raw_in = [sem(f"raw_in{i}") for i in range(4)]
        hi_done, lo_done, half_used = sem("hi_done"), sem("lo_done"), sem("half_used")
        masks_ready, setup_ready = sem("masks_ready"), sem("setup_ready")
        gT_ps, gT_ready = sem("gT_ps"), sem("gT_ready")
        xT_ps, x_ready = sem("xT_ps"), sem("x_ready")
        sq_ready, gh_ready, gl_ready, sacc_ready = sem("sq_ready"), sem("gh_ready"), sem("gl_ready"), sem("sacc_ready")
        stat_ps, var_ready, rstd_ready, r2T_ready = sem("stat_ps"), sem("var_ready"), sem("rstd_ready"), sem("r2T_ready")
        wf_hi, wf_lo, f_ps, f_chain, f_exp, F_ps, F_ready = (sem(n) for n in (
            "wf_hi", "wf_lo", "f_ps", "f_chain", "f_exp", "F_ps", "F_ready"))
        blk_ps, blk_evac, aug_done = sem("blk_ps"), sem("blk_evac"), sem("aug_done")
        st_out = [sem(f"st_out{i}") for i in range(4)]
        cka_ready, cka_out, lg_out = sem("cka_ready"), sem("cka_out"), sem("lg_out")
        nat_qk, nat_v = sem("nat_qk"), sem("nat_v")
        v_hi, v_split = sem("v_hi"), sem("v_split")
        s_ps, max_done, exp_done, recip_done, p_ready = (sem(n) for n in (
            "s_ps", "max_done", "exp_done", "recip_done", "p_ready"))
        g_ps, g_hi, g_lo = sem("g_ps"), sem("g_hi"), sem("g_lo")
        av_done, o_hi, o_lo, p_zero = sem("av_done"), sem("o_hi"), sem("o_lo"), sem("p_zero")
        wo_ps = sem("wo_ps")
        u_ps, u_relu, u_sq, u_hi, u_lo = (sem(n) for n in ("u_ps", "u_relu", "u_sq", "u_hi", "u_lo"))
        d_ps, acc_done, acc_scaled, x_d = sem("d_ps"), sem("acc_done"), sem("acc_scaled"), sem("x_d")
        z_ps, z_evac, z_sq, zv_ready, zr_ready, z_norm = (sem(n) for n in (
            "z_ps", "z_evac", "z_sq", "zv_ready", "zr_ready", "z_norm"))
        zT_ps, zT_hi, zT_lo, z_out = sem("zT_ps"), sem("zT_hi"), sem("zT_lo"), sem("z_out")
        lat_in, rope_in = sem("lat_in"), sem("rope_in")
        kr_chain, kr_ready, kr_ps, kr_T, kr_lo, rope_mul = (sem(n) for n in (
            "kr_chain", "kr_ready", "kr_ps", "kr_T", "kr_lo", "rope_mul"))
        lat_ps, lat_evac, lat_rope = sem("lat_ps"), sem("lat_evac"), sem("lat_rope")
        y_scaled, y_ps, y_evac, y_out = sem("y_scaled"), sem("y_ps"), sem("y_evac"), sem("y_out")
        y_outs = [y_out, sem("y_out1")]

        def piece_shape(j):
            if j < WO_A0:
                return 4, 512
            if KVD0 <= j < QD0:
                return 4, KVR + ROPE
            if QD0 <= j < KVU0:
                return 4, QR
            if KVU0 <= j < QU0:
                return 2, 1024
            if QU0 <= j < WO_B0:
                return 3, 384
            return 8, 256

        def piece_gain(j, k):
            if KVD0 <= j < QD0:
                return gT[:, 16 + 4 * (j - KVD0) + k:17 + 4 * (j - KVD0) + k]
            if QD0 <= j < KVU0:
                return gT[:, 24 + 4 * (j - QD0) + k:25 + 4 * (j - QD0) + k]
            return None

        def view(t, j):
            r, c = piece_shape(j)
            return t[:, j % 4, 0:r * c].rearrange("p (k c) -> p k c", c=c)

        V_COL, K_COL, Q_COL = 2 * D, D, 0
        BLOCKS = [("v", 0), ("v", 1), ("k", 0), ("k", 1), ("q", 0), ("q", 1)]

        def stored(slot, upto):
            n = 0
            for i in range(slot, upto, 4):
                kind = BLOCKS[i // 5][0]
                n += {"v": 1, "k": 2, "q": 1}[kind] + (i % 5 == NT and kind != "q")
            return 16 * n

        def block_col(b):
            kind, half = BLOCKS[b]
            return {"v": V_COL, "k": K_COL, "q": Q_COL}[kind] + 512 * half

        w_in = io["w_in_a"][0]

        def piece_src(j):
            if j < WO_A0:
                b, hf = j // 2, j % 2
                c = block_col(b)
                return w_in[512 * hf:512 * hf + 512, c:c + 512].rearrange("(k p) n -> p k n", p=P)
            if j < MLP_A0:
                c = CH * (j - WO_A0)
                return io["w_o_a"][0][:, c:c + CH].rearrange("(k p) n -> p k n", p=P)
            if j < QD0:
                r = 512 * (j - KVD0)
                return io["w_kv_down"][r:r + 512, :].rearrange("(k p) n -> p k n", p=P)
            if j < KVU0:
                r = 512 * (j - QD0)
                return io["w_q_down"][0][r:r + 512, :].rearrange("(k p) n -> p k n", p=P)
            if j < QU0:
                c = 1024 * (j - KVU0)
                return io["w_kv_up"][:, c:c + 1024].rearrange("(k p) n -> p k n", p=P)
            if j < WO_B0:
                c = 384 * (j - QU0)
                return io["w_q_up"][0][:, c:c + 384].rearrange("(k p) n -> p k n", p=P)
            c = CH * (j - WO_B0)
            return io["w_o_b"][0][:, c:c + CH].rearrange("(k p) n -> p k n", p=P)

        def up_src(layer, c):
            return io["w_up"][layer].rearrange("(k p) n -> p k n", p=P)[:, :, bass.ds(c * CH, CH)]

        def down_src(layer, c):
            return io["w_down"][layer].rearrange("(c k p) n -> c p k n", p=P, k=2)[c]

        def wait_tile(eng, b, t):
            if t < NT:
                eng.wait_ge(blk_ps, 4 * b + t + 1)
            else:
                eng.wait_ge(half_used, 2 * b + 2)

        def wait_lat(eng, n):
            if n < 28:
                eng.wait_ge(half_used, KVU0 + 1 + n // 14) if n % 14 == 13 else eng.wait_ge(lat_ps, n - n // 14 + 1)
            else:
                m = n - 28
                eng.wait_ge(half_used, QU0 + 1 + m // 5) if m % 5 == 4 else eng.wait_ge(lat_ps, 26 + m - m // 5 + 1)

        def mlp_views(t, j):
            up = t[:, j % 4, :].rearrange("p (k c) -> p k c", c=CH)
            down = t[:, j % 4, :].rearrange("p (k c) -> p k c", c=D)
            return up, down

        def p_group(u, part):
            def copies(bank, q_, k_, pt):
                if u == NT:
                    return [(pt[:, 2560:2800], ps[:, bank, 0:240])]
                n = min(u + 2, 4) if part == 0 else 1
                b0 = 0 if part == 0 else 4
                dst = pt[:, 0:2560].rearrange("p (b q) -> p b q", q=512)[:, b0:b0 + n, P * u:P * u + P]
                return [(dst, ps[:, bank, 0:P * n].rearrange("p (b q) -> p b q", q=P))]
            return copies

        S_COL = [0, 512, 1024, 0, 1024]
        P_PARTS = [(0, 0), (1, 0), (2, 0), (3, 0), (3, 1), (NT, 0)]

        def group_at(h, q):
            return h * 9 + (q - 6 if isinstance(h, int) and h == HEADS else q - 3)

        def prep_group(layer, q, slot):
            rq = R_FOX if layer == 0 else R_MLA
            rk = R_FOX if layer == 0 else HD

            def copies(bank, q_, k_, pt):
                if q == 0:
                    return [(q_[0:rq, slot, 0:SEQ], ps[0:rq, bank, 0:SEQ])]
                if q == 1:
                    return [(k_[0:rk, slot, 0:336], ps[0:rk, bank, 0:336]),
                            (q_[0:rq, slot, SEQ:T], ps[0:rq, bank, 336:416])]
                return [(k_[0:rk, slot, 336:KEYS], ps[0:rk, bank, 0:SEQ])]
            return copies

        okp, ovp = io["o_k_p"], io["o_v_p"]
        oks, ovs = io["o_k_s"], io["o_v_s"]

        def two_banks(pair, n):
            return ps[:, 2 * pair:2 * pair + 2, 0:n // 2]

        def halves(ap):
            return ap.rearrange("p (a b) -> p a b", a=2)

        block = ctx.enter_context(nc.Block())

        @block.sync
        def _(sp):
            def load(j):
                if j >= 4:
                    sp.wait_ge(lo_done, j - 3)
                r, c = piece_shape(j)
                sp.dma_start(view(raw, j), piece_src(j)).then_inc(raw_in[j % 4], 16)

            x = io["x_prompt"]
            sp.dma_start(cst[:], io["cst"]).then_inc(cst_in, 16)
            sp.dma_start(mraw[:], io["masks"]).then_inc(mask_in, 16)
            for i, g in enumerate((io["norm_mix"][0], io["norm_ffn"][0], io["kv_norm"], io["norm_mix"][1],
                                   io["norm_ffn"][1], io["final_norm"])):
                sp.dma_start(gn[8 * i:8 * i + 8, :], g.rearrange("(k p) -> k p", p=P)).then_inc(gain_in, 16)
            for t in range(NT):
                sp.dma_start(xn[:, t, :], x[P * t:P * t + P, :]).then_inc(x_in, 16)
            sp.dma_start(xn[0:SAM, NT, :], io["x_sample"]).then_inc(x_in, 16)
            sp.dma_start(xn[SAM:TX, NT, :], io["meta_tokens"]).then_inc(x_in, 16)
            sp.dma_start(wf[:], w_in[:, 3 * D:3 * D + HEADS].rearrange("(k p) n -> p k n", p=P)).then_inc(small_in, 16)
            sp.dma_start(bfb[:], io["b_f"].partition_broadcast(P)).then_inc(small_in, 16)
            sp.dma_start(lg[:, 5:7, :], io["cache_logf"].rearrange("(t p) h -> p t h", p=P)).then_inc(small_in, 16)
            sp.dma_start(ckn[:], io["cache_k"].rearrange("(t p) n -> p t n", p=P)).then_inc(small_in, 16)
            sp.wait_ge(masks_ready, 1)
            load(0)
            sp.wait_ge(gT_ps, 1)
            for j in range(1, 4):
                load(j)

            for b, (kind, hf) in enumerate(BLOCKS):
                for j in (2 * b + 4, 2 * b + 5):
                    load(j)
                if b == 2:
                    sp.wait_ge(F_ready, 1)
                    lgo = io["o_lf_p"]
                    sp.dma_start(lgo[META:, :].rearrange("(t p) h -> p t h", p=P), lg[:, 0:NT, :]).then_inc(lg_out, 16)
                    sp.dma_start(lgo[0:META, :], lg[SAM:TX, NT, :]).then_inc(lg_out, 16)
                    sp.dma_start(io["o_lf_s"], lg[0:SAM, NT, :]).then_inc(lg_out, 16)
                    sp.wait_ge(cka_ready, 2)
                    sp.dma_start(kscr[0][T:, :].rearrange("(t p) n -> p t n", p=P),
                                 cka[:, :, :, :].rearrange("p t h r -> p t (h r)")).then_inc(cka_out, 16)
                for t in range(5):
                    n = 5 * b + t
                    sp.wait_ge(blk_evac, n + 1)
                    if kind != "v":
                        sp.wait_ge(aug_done, n - 9)
                    done = st_out[n % 4]
                    cols = slice(512 * hf, 512 * hf + 512)
                    rows = slice(P * t, P * t + TILE_ROWS[t])
                    if kind == "v":
                        src = stg[:, n % 4, 0:512]
                        op, os_ = ovp, ovs
                    else:
                        scr = (kscr if kind == "k" else qscr)[0]
                        sp.dma_start(scr[rows, 528 * hf:528 * hf + 528],
                                     stg[0:TILE_ROWS[t], n % 4, :]).then_inc(done, 16)
                        if kind == "q":
                            continue
                        src = stg[:, n % 4, :].rearrange("p (h r) -> p h r", r=R_FOX)[:, :, 0:HD]
                        op, os_ = okp, oks

                    def dst(ap):
                        return ap if kind == "v" else ap.rearrange("p (h r) -> p h r", r=HD)
                    if t < NT:
                        sp.dma_start(dst(op[META + P * t:META + P * t + P, cols]), src).then_inc(done, 16)
                    else:
                        sp.dma_start(dst(os_[:, cols]), src[0:SAM]).then_inc(done, 16)
                        sp.dma_start(dst(op[0:META, cols]), src[SAM:TX]).then_inc(done, 16)

            def fox_qk(j):
                c = bass.ds(j * (2 * R_FOX), 2 * R_FOX)
                for scr, nat in ((qscr[0], natq[0]), (kscr[0], natk[0])):
                    sp.dma_start(nat[:, 0:NT, :], scr[0:SEQ, c].rearrange("(t p) n -> p t n", p=P)).then_inc(nat_qk, 16)
                    sp.dma_start(nat[0:TX, NT, :], scr[SEQ:T, c]).then_inc(nat_qk, 16)
                sp.dma_start(natk[0][:, 5:7, :], kscr[0][T:, c].rearrange("(t p) n -> p t n", p=P)).then_inc(nat_qk, 16)

            def fox_v(j):
                c = bass.ds(j * P, P)
                sp.dma_start(natv0[:, 0:NT, :], ovp[META:, c].rearrange("(t p) n -> p t n", p=P)).then_inc(nat_v, 16)
                sp.dma_start(natv0[0:SAM, NT, :], ovs[:, c]).then_inc(nat_v, 16)
                sp.dma_start(natv0[SAM:TX, NT, :], ovp[0:META, c]).then_inc(nat_v, 16)
                sp.dma_start(natv0[:, 5:7, :], io["cache_v"][:, c].rearrange("(t p) n -> p t n", p=P)).then_inc(nat_v, 16)

            def mla_qkv(j):
                c = bass.ds(j * (2 * R_MLA), 2 * R_MLA)
                sp.dma_start(natq[1][:, 0:NT, :], qscr[1][0:SEQ, c].rearrange("(t p) n -> p t n", p=P)).then_inc(nat_qk, 16)
                sp.dma_start(natq[1][0:TX, NT, :], qscr[1][SEQ:T, c]).then_inc(nat_qk, 16)
                c = bass.ds(j * (4 * HD), 4 * HD)
                sp.dma_start(natk[1][:, 0:NT, :], kscr[1][0:SEQ, c].rearrange("(t p) n -> p t n", p=P)).then_inc(nat_qk, 16)
                sp.dma_start(natk[1][0:TX, NT, :], kscr[1][SEQ:T, c]).then_inc(nat_qk, 16)
                sp.dma_start(natk[1][:, 5:7, :], kscr[1][T:, c].rearrange("(t p) n -> p t n", p=P)).then_inc(nat_qk, 16)

            for i in range(4):
                sp.wait_ge(st_out[i], stored(i, 30))
            sp.wait_ge(cka_out, 16)
            fox_qk(0)
            fox_v(0)
            with sp.Fori(0, PAIRS - 1) as i:
                sp.wait_ge(g_ps, i * 18 + 6)
                fox_qk(i + 1)
                sp.wait_ge(v_split, i + 1)
                fox_v(i + 1)
                sp.nop()

            def mlp_loads(layer, j0):
                def mload(j, src_of_up, c, n=0):
                    up, down = mlp_views(raw, j)
                    sp.wait_ge(lo_done, (j - 3) + 4 * n)
                    if src_of_up:
                        sp.dma_start(up, up_src(layer, c)).then_inc(raw_in[j % 4], 16)
                    else:
                        sp.dma_start(down, down_src(layer, c)).then_inc(raw_in[j % 4], 16)
                mload(j0, True, 0)
                with sp.Fori(0, NCH // 2 - 1) as i:
                    mload(j0 + 1, True, 2 * i + 1, i)
                    mload(j0 + 2, False, 2 * i, i)
                    mload(j0 + 3, True, 2 * i + 2, i)
                    mload(j0 + 4, False, 2 * i + 1, i)
                    sp.nop()
                mload(j0 + 29, True, NCH - 1)
                mload(j0 + 30, False, NCH - 2)
                mload(j0 + 31, False, NCH - 1)

            mlp_loads(0, MLP_A0)

            for j in range(KVD0, QU0):
                load(j)
            sp.wait_ge(x_ready, 24)
            sp.dma_start(zc[:, 5:7, :], io["cache_ckv"].rearrange("(t p) n -> p t n", p=P)).then_inc(lat_in, 16)
            sp.dma_start(gckv[:], io["ckv_norm"].partition_broadcast(P)).then_inc(lat_in, 16)
            sp.wait_ge(half_used, KVU0)
            sp.dma_start(krn[:, 5:7, :], io["cache_kr"].rearrange("(t p) n -> p t n", p=P)).then_inc(rope_in, 16)
            sp.dma_start(gq[:], io["q_norm"].partition_broadcast(P)).then_inc(rope_in, 16)
            for j in range(QU0, WO_B0):
                load(j)
            sp.wait_ge(z_norm, 5)
            ckp = io["o_ckv_p"]
            sp.dma_start(ckp[META:, :].rearrange("(t p) n -> p t n", p=P), zc[:, 0:NT, :]).then_inc(z_out, 16)
            sp.dma_start(io["o_ckv_s"], zc[0:SAM, NT, :]).then_inc(z_out, 16)
            sp.dma_start(ckp[0:META, :], zc[SAM:TX, NT, :]).then_inc(z_out, 16)
            sp.wait_ge(kr_ready, 1)
            krp = io["o_kr_p"]
            sp.dma_start(krp[META:, :].rearrange("(t p) n -> p t n", p=P), krn[:, 0:NT, :]).then_inc(z_out, 16)
            sp.dma_start(io["o_kr_s"], krn[0:SAM, NT, :]).then_inc(z_out, 16)
            sp.dma_start(krp[0:META, :], krn[SAM:TX, NT, :]).then_inc(z_out, 16)
            for n in range(28):
                t, blk = (n % 14) // 2, 2 * (n // 14) + n % 2
                rows = P if t != NT else TX
                r0 = P * t if t <= NT else T + P * (t - 5)
                sp.wait_ge(lat_evac, n + 1)
                sp.dma_start(kscr[1][r0:r0 + rows, 512 * blk:512 * blk + 512],
                             stn[0:rows, n % 4, :]).then_inc(st_out[n % 4], 16)
            for n in range(20):
                t, g = n % 5, n // 5
                sp.wait_ge(lat_rope, n + 1)
                sp.dma_start(qscr[1][P * t:P * t + TILE_ROWS[t], 384 * g:384 * g + 384],
                             stn[0:TILE_ROWS[t], n % 4, 0:384]).then_inc(st_out[n % 4], 16)
            for j in range(WO_B0, MLP_B0):
                load(j)
            for i in range(4):
                sp.wait_ge(st_out[i], stored(i, 30) + 16 * 12)
            sp.wait_ge(z_out, 96)
            mla_qkv(0)
            with sp.Fori(0, PAIRS - 1) as i:
                sp.wait_ge(v_split, i + 1 + PAIRS)
                sp.wait_ge(g_ps, i * 18 + (9 * HEADS + 6))
                mla_qkv(i + 1)
                sp.nop()
            mlp_loads(1, MLP_B0)
            for t in range(5):
                sp.wait_ge(y_evac, t + 1)
                if t < NT:
                    sp.dma_start(io["y_p"][P * t:P * t + P, :], yst[:, t % 2, :]).then_inc(y_outs[t % 2], 16)
                else:
                    sp.dma_start(io["y_s"], yst[0:SAM, t % 2, :]).then_inc(y_outs[t % 2], 16)
            sp.wait_ge(y_outs[0], 48)
            sp.wait_ge(y_outs[1], 32)
            sp.wait_ge(z_out, 96)
            sp.wait_ge(lg_out, 48)

        @block.gpsimd
        def _(pool):
            g = nc.gpsimd
            g.memset(mhalf[:], -0.5).then_inc(setup_ready, 1)
            g.memset(sacc[:, T:5 * P], 1.0).then_inc(setup_ready, 1)
            g.memset(ss[:], 1.0).then_inc(setup_ready, 1)

            def add_squares(b, k):
                pool.wait_ge(sq_ready, KD * b + k + 1)
                if k > 1:
                    pool.wait_ge(sacc_ready, 7 * b + k - 1)
                g.tensor_tensor(sacc[:, 0:T], sacc[:, 0:T], sq[:, k % 2, :], ALU.add).then_inc(sacc_ready, 1)

            def sum_squares(b):
                for k in range(1, KD):
                    add_squares(b, k)

            def rstd(n):
                pool.wait_ge(var_ready, n + 1)
                g.tensor_tensor(rst[:], v5[:], mhalf[:], ALU.pow).then_inc(rstd_ready, 1)

            pool.wait_ge(setup_ready, 3)
            sum_squares(0)
            rstd(0)
            pool.wait_ge(small_in, 64)
            g.tensor_copy(cka[:, :, :, 0:HD], ckn[:, :, :].rearrange("p t (h r) -> p t h r", r=HD)).then_inc(cka_ready, 1)
            pool.wait_ge(F_ready, 1)
            g.tensor_copy(cka[:, :, :, HD:R_FOX], FK[:, 5:7, :, :]).then_inc(cka_ready, 1)
            for n in range(10, 30):
                kind, hf = BLOCKS[n // 5]
                t = n % 5
                pool.wait_ge(st_out[n % 4], stored(n % 4, n - 3))
                tab = FK if kind == "k" else FQ
                g.tensor_copy(stg[:, n % 4, :].rearrange("p (h r) -> p h r", r=R_FOX)[0:TILE_ROWS[t], :, HD:R_FOX],
                              tab[0:TILE_ROWS[t], t, 8 * hf:8 * hf + 8, :]).then_inc(aug_done, 1)

            def split_v(layer, j, after_av=True):
                if layer == 0:
                    pool.wait_ge(nat_v, j * 64 + 64)
                else:
                    pool.wait_ge(nat_qk, j * 80 + 80 + 80 * PAIRS)
                if after_av:
                    pool.wait_ge(av_done, j * 2 + HEADS * layer)
                views = []
                for t0, t1, rows in ((NT, 5, TX), (0, NT, P), (5, 7, P)):
                    if layer == 0:
                        src = natv0[0:rows, t0:t1, :].rearrange("p t (h d) -> p t h d", h=2)
                    else:
                        src = natk[1][0:rows, t0:t1, :].rearrange("p t (h d) -> p t h d", h=2)[:, :, :, HD:2 * HD]
                    views.append((src, slice(0, rows), slice(t0, t1)))
                src, r, t = views[0]
                g.tensor_tensor(vh[r, NT, :].rearrange("p (h d) -> p h d", h=2), src.rearrange("p t h d -> p (t h) d"),
                                ones[r, :].rearrange("p (h d) -> p h d", h=2), ALU.mult).then_inc(v_hi, 1)
                for src, r, t in views[1:]:
                    g.tensor_copy(vh[r, t, :].rearrange("p t (h d) -> p t h d", h=2), src).then_inc(v_hi, 1)
                pool.wait_ge(v_hi, j * 3 + 3 + 3 * PAIRS * layer)
                for n, (src, r, t) in enumerate(views):
                    i = g.tensor_tensor(vl[r, t, :].rearrange("p t (h d) -> p t h d", h=2), src,
                                        vh[r, t, :].bitcast(F32).rearrange("p t (h d) -> p t h d", h=2), ALU.subtract)
                i.then_inc(v_split, 1)

            split_v(0, 0, False)
            with pool.Fori(1, PAIRS) as j:
                split_v(0, j)

            def mlp_finish(layer):
                n = T if layer == 0 else T1
                pool.wait_ge(r2T_ready, layer + 1)
                for m in range(KD + 2):
                    if m < KD:
                        pool.wait_ge(acc_done, ACC_N * (layer + 1) - KD + m + 1)
                        g.tensor_tensor(acc[:, m, 0:n], acc[:, m, 0:n], r2T[:, 0:n], ALU.mult).then_inc(acc_scaled, 1)
                    if m > 2:
                        add_squares(2 * layer + 2, m - 2)

            sum_squares(1)
            mlp_finish(0)
            rstd(1)
            for i in range(2):
                pool.wait_ge(zv_ready, i + 1)
                g.tensor_tensor(rc[:, i, :], ss[:, i, :], mhalf[:], ALU.pow).then_inc(zr_ready, 1)
            for n in range(20):
                t = n % 5
                r = TILE_ROWS[t]
                v = stn[0:r, (n + 28) % 4, 0:384].rearrange("p (h c) -> p h c", c=R_MLA)
                x1, x2 = v[:, :, HD:HD + 16], v[:, :, HD + 16:R_MLA]
                cos = cst[0:r, C_COS + 16 * t:C_COS + 16 * t + 16].unsqueeze(1).to_broadcast([r, 4, 16])
                sin = cst[0:r, C_SIN + 16 * t:C_SIN + 16 * t + 16].unsqueeze(1).to_broadcast([r, 4, 16])
                pool.wait_ge(lat_evac, 28 + n + 1)
                if n:
                    pool.wait_ge(lat_rope, n)
                for i, (a, b) in enumerate(((x1, cos), (x2, sin), (x2, cos), (x1, sin))):
                    g.tensor_tensor(rtmp[0:r, i, :, :], a, b, ALU.mult).then_inc(rope_mul, 1)
                pool.wait_ge(rope_mul, 4 * n + 4)
                g.tensor_tensor(x1, rtmp[0:r, 0, :, :], rtmp[0:r, 1, :, :], ALU.subtract)
                g.tensor_tensor(x2, rtmp[0:r, 2, :, :], rtmp[0:r, 3, :, :], ALU.add).then_inc(lat_rope, 1)
            split_v(1, 0, False)
            with pool.Fori(1, PAIRS) as j:
                split_v(1, j)
            sum_squares(3)
            mlp_finish(1)
            rstd(2)

        @block.scalar
        def _(act):
            s = nc.scalar

            def hi(j, n=0, waits=True):
                act.wait_ge(raw_in[j % 4], 16 * (j // 4 + 1) + 16 * n)
                if j >= 4:
                    act.wait_ge(half_used, j - 3 + 4 * n)
                if piece_gain(j, 0) is None:
                    r, c = piece_shape(j)
                    s.activation(wh[:, j % 4, 0:r * c], raw[:, j % 4, 0:r * c], ACT.Copy).then_inc(hi_done, 1)
                else:
                    a, b = view(wh, j), view(raw, j)
                    for k in range(4):
                        i = s.activation(a[:, k, :], b[:, k, :], ACT.Copy, scale=piece_gain(j, k))
                    i.then_inc(hi_done, 1)

            def square_and_gain(b, gain, pieces=None):
                for k in range(KD):
                    act.wait_ge(x_ready, KD * b + k + 1)
                    if k == 0 and b:
                        act.wait_ge(stat_ps, b)
                    if k >= 1 and 7 * b + max(k - 2, 0) > 0:
                        act.wait_ge(sacc_ready, 7 * b + max(k - 2, 0))
                    dst = sacc[:, 0:T] if k == 0 else sq[:, k % 2, :]
                    s.activation(dst, xT[:, k, :], ACT.Square).then_inc(sq_ready, 1)
                    if gain is None:
                        s.activation(xgh[:, k, :], xT[:, k, :], ACT.Copy).then_inc(gh_ready, 1)
                    elif b < 4:
                        s.activation(xgh[:, k, :], xT[:, k, :], ACT.Copy,
                                     scale=gT[:, gain + k:gain + k + 1]).then_inc(gh_ready, 1)
                    else:
                        s.activation(yT[:, k, :], xT[:, k, 0:T1], ACT.Copy,
                                     scale=gT[:, gain + k:gain + k + 1]).then_inc(y_scaled, 1)
                    if pieces is not None and k in (2, 4, 6):
                        hi(pieces + k // 2 - 1)

            act.wait_ge(gT_ready, 1)
            act.wait_ge(setup_ready, 3)
            square_and_gain(0, 0)
            act.wait_ge(small_in, 64)
            s.activation(wfh[:], wf[:], ACT.Copy).then_inc(wf_hi, 1)
            for j in range(4):
                hi(j)
            act.wait_ge(f_chain, 3)
            s.activation(ft[:, 2, :], ft[:, 1, :], ACT.Exp, scale=-1.0).then_inc(f_exp, 1)
            act.wait_ge(rstd_ready, 2)
            for b, (kind, hf) in enumerate(BLOCKS):
                for t in range(5):
                    n = 5 * b + t
                    r = TILE_ROWS[t]
                    wait_tile(act, b, t)
                    if n >= 4:
                        act.wait_ge(st_out[n % 4], stored(n % 4, n - 3))
                    src = ps[0:r, n % 4, :]
                    if kind == "v":
                        dst = stg[0:r, n % 4, 0:512]
                    else:
                        src = src.rearrange("p (h d) -> p h d", d=HD)
                        dst = stg[0:r, n % 4, :].rearrange("p (h d) -> p h d", d=R_FOX)[:, :, 0:HD]
                    sc = (rst8 if kind == "q" else rst)[0:r, t:t + 1]
                    s.activation(dst, src, ACT.Copy, scale=sc).then_inc(blk_evac, 1)
                if b < 4:
                    hi(2 * b + 4)
                    hi(2 * b + 5)

            def attention(layer):
                U0, G0, H0 = 5 * HEADS * layer, 9 * HEADS * layer, HEADS * layer

                def exp(h, c, u):
                    n = unit_keys(u)[1]
                    rows = P if u < NT else TX
                    off = P_OFF[u] + (64 if u < NT else 0)
                    act.wait_ge(max_done, h * 5 + (U0 + u + 1))
                    s.activation(prob[0:rows, c, off:off + n], pf[0:rows, S_COL[u]:S_COL[u] + n], ACT.Exp,
                                 bias=nmx[0:rows, u:u + 1], accum_out=sm[0:rows, u:u + 1]).then_inc(exp_done, 1)

                def group(h, q, what):
                    act.wait_ge(g_ps, group_at(h, q) + (G0 + 1))
                    copies = what(3 + q % 3, qh, kh, pth)
                    for dst, src in copies[:-1]:
                        s.activation(dst, src, ACT.Copy)
                    dst, src = copies[-1]
                    s.activation(dst, src, ACT.Copy).then_inc(g_hi, 1)

                def turned(h, q):
                    group(h, q, p_group(*P_PARTS[q]))

                def out(head, p, pair):
                    act.wait_ge(av_done, head + (H0 + 1))
                    s.activation(oh[64 * p:64 * p + 64, pair, :], pf[64 * p:64 * p + 64, 3072:3072 + T],
                                 ACT.Copy).then_inc(o_hi, 1)

                def step(h, c, pair, first=False, last=False):
                    if not first:
                        turned(h, 0)
                        turned(h, 1)
                    exp(h, c, 0)
                    if not first:
                        turned(h, 2)
                    exp(h, c, 1)
                    if not first:
                        turned(h, 3)
                    exp(h, c, 2)
                    if not first:
                        turned(h, 4)
                        if not (isinstance(h, int) and h == 1):
                            out(h - 2, c, pair - 1)
                        turned(h, 5)
                    exp(h, c, 3)
                    if not last:
                        group(h, 6, prep_group(layer, 0, 1 - c))
                    exp(h, c, 4)
                    if not last:
                        group(h, 7, prep_group(layer, 1, 1 - c))
                        group(h, 8, prep_group(layer, 2, 1 - c))

                for q in range(3):
                    group(-1, 6 + q + 6, prep_group(layer, q, 0))
                step(0, 0, 0, first=True)
                step(1, 1, 0)
                with act.Fori(1, PAIRS - 1) as i:
                    step(2 * i, 0, i)
                    step(2 * i + 1, 1, i)
                step(HEADS - 2, 0, PAIRS - 1)
                step(HEADS - 1, 1, PAIRS - 1, last=True)
                for q in range(6):
                    turned(HEADS, q)
                    if q == 1:
                        out(HEADS - 2, 0, PAIRS - 1)
                out(HEADS - 1, 1, PAIRS - 1)

            attention(0)

            for q in range(4):
                hi(WO_A0 + q)
            square_and_gain(1, 8, MLP_A0)

            def mlp(layer, j0, tail):
                n = T if layer == 0 else T1
                cnt = 2 * NCH * layer

                def hidden(c, par_c, used):
                    for m in range(2):
                        v = two_banks(m, n)
                        if m == 0:
                            act.wait_ge(u_ps, c + 1 + NCH * layer)
                        else:
                            act.wait_ge(half_used, used)
                        s.activation(v, v, ACT.Relu).then_inc(u_relu, 1)
                        act.wait_ge(u_relu, c * 2 + m + 1 + cnt)
                        s.activation(v, v, ACT.Square).then_inc(u_sq, 1)
                        act.wait_ge(u_sq, c * 2 + m + 1 + cnt)
                        s.activation(halves(hh[:, par_c, m, 0:n]), v, ACT.Copy).then_inc(u_hi, 1)

                hidden(0, 0, j0 + 1)
                with act.Fori(0, NCH // 2 - 1) as i:
                    for q in range(2):
                        hi(j0 + 2 * q + 3, i)
                        hi(j0 + 2 * q + 4, i)
                        hidden(2 * i + q + 1, (q + 1) % 2, 4 * i + (j0 + 2 * q + 2))
                hi(j0 + 31)
                if tail:
                    hi(j0 + 32)
                hidden(NCH - 1, 1, j0 + 30)
                if tail:
                    hi(j0 + 33)
                    hi(j0 + 34)

            mlp(0, MLP_A0, True)
            square_and_gain(2, None)
            hi(QD0 + 1)
            for t in range(5):
                act.wait_ge(z_evac, 2 * t + 1)
                act.wait_ge(sacc_ready, 21)
                if t >= 2:
                    act.wait_ge(z_sq, t - 1)
                s.activation(sq[0:TILE_ROWS[t], t % 2, 0:KVR], zc[0:TILE_ROWS[t], t, :], ACT.Square,
                             accum_out=ss[0:TILE_ROWS[t], 0, t:t + 1]).then_inc(z_sq, 1)
            hi(KVU0)
            hi(KVU0 + 1)
            for t in range(5):
                act.wait_ge(z_evac, 10 + t + 1)
                act.wait_ge(z_sq, 5 + t - 1)
                s.activation(sq[0:TILE_ROWS[t], t % 2, 0:QR], zq[0:TILE_ROWS[t], t, :], ACT.Square,
                             accum_out=ss[0:TILE_ROWS[t], 1, t:t + 1]).then_inc(z_sq, 1)
            for f in range(2):
                act.wait_ge(zT_ps, f + 1)
                s.activation(ckvTh[:, f, :], pf[:, 1024 * f:1024 * f + KEYS], ACT.Copy).then_inc(zT_hi, 1)
            hi(QU0)
            hi(QU0 + 1)
            for n in range(48):
                if n == 28:
                    act.wait_ge(z_out, 96)
                    for f in range(3):
                        act.wait_ge(zT_ps, f + 3)
                        c = 2048 + 1024 * (f % 2)
                        s.activation(cqTh[:, f, :], pf[:, c:c + T], ACT.Copy).then_inc(zT_hi, 1)
                wait_lat(act, n)
                if n >= 4:
                    act.wait_ge(st_out[n % 4], stored(n % 4, 30) + 16 * (n // 4))
                if n < 28:
                    t = (n % 14) // 2
                    r = TX if t == NT else P
                    s.activation(stn[0:r, n % 4, :], ps[0:r, n % 4, :], ACT.Copy).then_inc(lat_evac, 1)
                else:
                    r = TILE_ROWS[(n - 28) % 5]
                    s.activation(stn[0:r, n % 4, 0:384], ps[0:r, n % 4, 0:384], ACT.Copy,
                                 scale=MLA_SCALE).then_inc(lat_evac, 1)
                if n == 13:
                    hi(QU0 + 2)
                if n == 27:
                    hi(QU0 + 3)
            act.wait_ge(kr_ps, 1)
            for sl in range(2):
                s.activation(kh[HD:R_MLA, sl, 336:KEYS], pf[0:ROPE, 3072:3584], ACT.Copy)
                i = s.activation(kh[HD:R_MLA, sl, 0:336], pf[0:ROPE, 3584:3920], ACT.Copy)
            i.then_inc(kr_T, 1)
            attention(1)
            for q in range(4):
                hi(WO_B0 + q)
            square_and_gain(3, 32, MLP_B0)
            mlp(1, MLP_B0, False)
            square_and_gain(4, 40)
            for t in range(5):
                r = P if t < NT else SAM
                act.wait_ge(y_ps, t + 1)
                act.wait_ge(rstd_ready, 4)
                if t >= 2:
                    act.wait_ge(y_outs[t % 2], 16 * (t // 2))
                s.activation(yst[0:r, t % 2, :], pf[0:r, 1024 * (t % 2):1024 * (t % 2) + D], ACT.Copy,
                             scale=rst[0:r, t:t + 1]).then_inc(y_evac, 1)

        @block.vector
        def _(dve):
            v = nc.vector
            chained = [0]

            def link(i):
                chained[0] += 1
                i.then_inc(f_chain, 1)
                dve.wait_ge(f_chain, chained[0])

            def lo(j, n=0):
                dve.wait_ge(raw_in[j % 4], 16 * (j // 4 + 1) + 16 * n)
                dve.wait_ge(hi_done, j + 1 + 4 * n)
                if piece_gain(j, 0) is None:
                    r, c = piece_shape(j)
                    v.tensor_tensor(wl[:, j % 4, 0:r * c], raw[:, j % 4, 0:r * c],
                                    wh[:, j % 4, 0:r * c].bitcast(F32), ALU.subtract).then_inc(lo_done, 1)
                else:
                    a, b, w = view(wl, j), view(raw, j), view(wh, j)
                    for k in range(4):
                        i = v.scalar_tensor_tensor(a[:, k, :], b[:, k, :], piece_gain(j, k),
                                                   w[:, k, :].bitcast(F32), ALU.mult, ALU.subtract)
                    i.then_inc(lo_done, 1)

            def gain_lo(b, k, gain):
                dve.wait_ge(x_ready, KD * b + k + 1)
                dve.wait_ge(gh_ready, KD * b + k + 1)
                if gain is None:
                    v.tensor_tensor(xgl[:, k, :], xT[:, k, :], xgh[:, k, :].bitcast(F32),
                                    ALU.subtract).then_inc(gl_ready, 1)
                else:
                    v.scalar_tensor_tensor(xgl[:, k, :], xT[:, k, :], gT[:, gain + k:gain + k + 1],
                                           xgh[:, k, :].bitcast(F32), ALU.mult, ALU.subtract).then_inc(gl_ready, 1)

            def variance(b, bank):
                dve.wait_ge(stat_ps, b + 1)
                v.tensor_scalar(v5[:], ps[:, bank, 0:5], 1.0 / D, EPS, ALU.mult, ALU.add).then_inc(var_ready, 1)

            dve.wait_ge(mask_in, 16)
            v.tensor_copy(mask[:], mraw[:]).then_inc(masks_ready, 1)
            dve.wait_ge(cst_in, 16)
            v.tensor_copy(idr[:], ident).then_inc(masks_ready, 1)
            dve.wait_ge(gT_ps, 1)
            v.tensor_copy(gT[:], ps[:, 6, 0:48]).then_inc(gT_ready, 1)
            for k in range(KD + 1):
                if k < KD:
                    dve.wait_ge(xT_ps, k + 1)
                    c = 1024 * (k % 4)
                    v.tensor_copy(xT[:, k, :], pf[:, c:c + T]).then_inc(x_ready, 1)
                if k >= 1:
                    gain_lo(0, k - 1, 0)
            dve.wait_ge(wf_hi, 1)
            v.tensor_tensor(wfl[:], wf[:], wfh[:].bitcast(F32), ALU.subtract).then_inc(wf_lo, 1)
            variance(0, 6)
            dve.wait_ge(rstd_ready, 1)
            v.tensor_scalar(rst8[:], rst[:], FOX_SCALE, None, ALU.mult).then_inc(rstd_ready, 1)
            lo(0)
            lo(1)

            dve.wait_ge(small_in, 64)
            dve.wait_ge(f_ps, 1)
            z = lg[:, 0:5, :].rearrange("p t h -> p (t h)")
            link(v.memset(lg[:, 0:5, :], 0.0))
            for t in range(5):
                r = TILE_ROWS[t]
                i = v.scalar_tensor_tensor(lg[0:r, t, :], ps[0:r, 7, 16 * t:16 * t + 16], rst[0:r, t:t + 1],
                                           bfb[0:r, :], ALU.mult, ALU.add)
            link(i)
            link(v.scalar_tensor_tensor(ft[:, 1, :], z, -1.0, z, ALU.mult, ALU.max))
            dve.wait_ge(f_exp, 1)
            link(v.tensor_scalar(ft[:, 3, :], ft[:, 2, :], 2.0, None, ALU.add))
            link(v.reciprocal(ft[:, 4, :], ft[:, 3, :]))
            link(v.tensor_tensor(ft[:, 0, :], ft[:, 2, :], ft[:, 4, :], ALU.mult))
            link(v.tensor_tensor(ft[:, 3, :], ft[:, 0, :], ft[:, 0, :], ALU.mult))
            link(v.tensor_scalar(ft[:, 4, :], ft[:, 3, :], 1.0 / 17, None, ALU.mult))
            for c in (15, 13, 11, 9, 7, 5, 3):
                link(v.scalar_tensor_tensor(ft[:, 4, :], ft[:, 4, :], 1.0 / c, ft[:, 3, :], ALU.add, ALU.mult))
            link(v.scalar_tensor_tensor(ft[:, 5, :], ft[:, 4, :], 1.0, ft[:, 0, :], ALU.add, ALU.mult))
            link(v.tensor_scalar(ft[:, 1, :], z, 0.0, None, ALU.min))
            link(v.scalar_tensor_tensor(z, ft[:, 5, :], -2.0, ft[:, 1, :], ALU.mult, ALU.add))
            assert chained[0] == F_CHAIN
            lo(2)
            lo(3)
            link(v.memset(FQ[:], 1.0))
            link(v.memset(FK[:], 1.0))
            dve.wait_ge(F_ps, 1)
            fp = ps[:, 5, 0:112].rearrange("p (t h) -> p t h", h=HEADS)
            for t, r in ((slice(0, NT), P), (slice(NT, 5), TX)):
                v.tensor_copy(FQ[0:r, t, :, 1], fp[0:r, t, :])
                v.tensor_scalar(FK[0:r, t, :, 0], fp[0:r, t, :], -1.0, None, ALU.mult)
            v.tensor_scalar(FK[:, 5:7, :, 0], fp[:, 5:7, :], -1.0, None, ALU.mult).then_inc(F_ready, 1)
            for j in range(4, 12):
                lo(j)

            def attention(layer):
                U0, G0, H0 = 5 * HEADS * layer, 9 * HEADS * layer, HEADS * layer

                def row_max(h, u):
                    n = unit_keys(u)[1]
                    rows = P if u < NT else TX
                    dve.wait_ge(s_ps, h * 5 + (U0 + u + 1))
                    v.tensor_reduce(nmx[0:rows, u:u + 1], pf[0:rows, S_COL[u]:S_COL[u] + n], AX.X, ALU.max,
                                    negate=True).then_inc(max_done, 1)

                def normalise(h, c, u):
                    n = unit_keys(u)[1]
                    rows = P if u < NT else TX
                    off = P_OFF[u] + (64 if u < NT else 0)
                    dve.wait_ge(exp_done, h * 5 + (U0 + u + 1))
                    v.reciprocal(rs[0:rows, u:u + 1], sm[0:rows, u:u + 1]).then_inc(recip_done, 1)
                    dve.wait_ge(recip_done, h * 5 + (U0 + u + 1))
                    v.tensor_scalar(prob[0:rows, c, off:off + n], prob[0:rows, c, off:off + n], rs[0:rows, u:u + 1],
                                    None, ALU.mult).then_inc(p_ready, 1)

                def group(h, q, what):
                    bank = 3 + q % 3
                    dve.wait_ge(g_hi, group_at(h, q) + (G0 + 1))
                    both = list(zip(what(bank, ql, kl, ptl), what(bank, qh, kh, pth)))
                    for (dst, src), (hi_part, _) in both[:-1]:
                        v.tensor_tensor(dst, src, hi_part.bitcast(F32), ALU.subtract)
                    (dst, src), (hi_part, _) = both[-1]
                    v.tensor_tensor(dst, src, hi_part.bitcast(F32), ALU.subtract).then_inc(g_lo, 1)

                def turned(h, q):
                    group(h, q, p_group(*P_PARTS[q]))

                def out(head, p, pair):
                    rows = slice(64 * p, 64 * p + 64)
                    dve.wait_ge(o_hi, head + (H0 + 1))
                    v.tensor_tensor(ol[rows, pair, :], pf[rows, 3072:3072 + T], oh[rows, pair, :].bitcast(F32),
                                    ALU.subtract).then_inc(o_lo, 1)

                def step(h, c, pair, first=False, last=False):
                    if not first:
                        turned(h, 0)
                    row_max(h, 0)
                    if not first:
                        turned(h, 1)
                        normalise(h - 1, 1 - c, 4)
                    row_max(h, 1)
                    if not first:
                        turned(h, 2)
                    normalise(h, c, 0)
                    row_max(h, 2)
                    if not first:
                        turned(h, 3)
                    normalise(h, c, 1)
                    if not first:
                        turned(h, 4)
                    normalise(h, c, 2)
                    row_max(h, 3)
                    if not first:
                        if not (isinstance(h, int) and h == 1):
                            out(h - 2, c, pair - 1)
                        turned(h, 5)
                    row_max(h, 4)
                    if not last:
                        group(h, 6, prep_group(layer, 0, 1 - c))
                    normalise(h, c, 3)
                    if not last:
                        group(h, 7, prep_group(layer, 1, 1 - c))
                        group(h, 8, prep_group(layer, 2, 1 - c))

                dve.wait_ge(half_used, WO_A0 if layer == 0 else WO_B0)
                for u in range(NT):
                    v.memset(prob[:, :, P_OFF[u]:P_OFF[u] + 64], 0.0)
                v.memset(prob[:, :, P_OFF[NT] + 336:P_OFF[NT] + 384], 0.0).then_inc(p_zero, 1)
                if layer == 1:
                    dve.wait_ge(kr_T, 1)
                    for sl in range(2):
                        v.tensor_tensor(kl[HD:R_MLA, sl, 336:KEYS], pf[0:ROPE, 3072:3584],
                                        kh[HD:R_MLA, sl, 336:KEYS].bitcast(F32), ALU.subtract)
                        i = v.tensor_tensor(kl[HD:R_MLA, sl, 0:336], pf[0:ROPE, 3584:3920],
                                            kh[HD:R_MLA, sl, 0:336].bitcast(F32), ALU.subtract)
                    i.then_inc(kr_lo, 1)
                for q in range(3):
                    group(-1, 6 + q + 6, prep_group(layer, q, 0))
                step(0, 0, 0, first=True)
                step(1, 1, 0)
                with dve.Fori(1, PAIRS - 1) as i:
                    step(2 * i, 0, i)
                    step(2 * i + 1, 1, i)
                step(HEADS - 2, 0, PAIRS - 1)
                step(HEADS - 1, 1, PAIRS - 1, last=True)
                for q in range(6):
                    turned(HEADS, q)
                    if q == 1:
                        out(HEADS - 2, 0, PAIRS - 1)
                        normalise(HEADS - 1, 1, 4)
                out(HEADS - 1, 1, PAIRS - 1)

            def residual_and_gain(b, j0, gain, n):
                for m in range(KD + 1):
                    if m < KD:
                        if m % 2:
                            dve.wait_ge(half_used, j0 + m // 2 + 1)
                        else:
                            dve.wait_ge(wo_ps, 4 * (b // 2) + m // 2 + 1)
                        a = halves(xT[:, m, 0:n])
                        v.tensor_tensor(a, a, two_banks(m % 2, n), ALU.add).then_inc(x_ready, 1)
                    if m in (2, 4, 6):
                        lo(j0 + 4 + m // 2 - 1)
                    if m >= 1:
                        gain_lo(b, m - 1, gain)

            def mlp(layer, j0, gain, tail):
                n = T if layer == 0 else T1
                b = 2 * layer + 2

                def hidden(c, par_c):
                    for m in range(2):
                        dve.wait_ge(u_hi, c * 2 + (m + 1 + 2 * NCH * layer))
                        v.tensor_tensor(halves(hl[:, par_c, m, 0:n]), two_banks(m, n),
                                        halves(hh[:, par_c, m, 0:n].bitcast(F32)), ALU.subtract).then_inc(u_lo, 1)

                def add(c, m, used):
                    if m < KD - 1:
                        dve.wait_ge(d_ps, c * 7 + (m + 1 + 7 * NCH * layer))
                    else:
                        dve.wait_ge(half_used, used)
                    dve.wait_ge(acc_done, c * KD + (m + 1 + ACC_N * layer))
                    a = halves(acc[:, m, 0:n])
                    v.tensor_tensor(a, a, two_banks(2 + m % 2, n), ALU.add).then_inc(acc_done, 1)

                dve.wait_ge(stat_ps, 2 * layer + 2)
                v.tensor_scalar(r2T[:], pf[:, 3072:3072 + T], 1.0 / D, EPS, ALU.mult, ALU.add).then_inc(x_d, 1)
                dve.wait_ge(x_d, layer + 1)
                v.reciprocal(r2T[:], r2T[:]).then_inc(r2T_ready, 1)
                dve.wait_ge(half_used, j0)
                for m in range(KD):
                    v.memset(acc[:, m, :], 0.0).then_inc(acc_done, 1)
                hidden(0, 0)
                with dve.Fori(0, NCH // 2 - 1) as i:
                    for q in range(2):
                        lo(j0 + 2 * q + 3, i)
                        lo(j0 + 2 * q + 4, i)
                        hidden(2 * i + q + 1, (q + 1) % 2)
                        for m in range(KD):
                            add(2 * i + q, m, 4 * i + (j0 + 2 * q + 3))
                lo(j0 + 31)
                if tail:
                    lo(j0 + 32)
                hidden(NCH - 1, 1)
                for m in range(KD):
                    add(NCH - 2, m, j0 + 31)
                if tail:
                    lo(j0 + 33)
                    lo(j0 + 34)
                for m in range(KD + 3):
                    if m < KD:
                        add(NCH - 1, m, j0 + 32)
                    if 1 <= m <= KD:
                        dve.wait_ge(acc_scaled, KD * layer + m)
                        v.tensor_tensor(xT[:, m - 1, 0:n], xT[:, m - 1, 0:n], acc[:, m - 1, 0:n],
                                        ALU.add).then_inc(x_ready, 1)
                    if 3 <= m and layer == 0:
                        gain_lo(b, m - 3, gain)

            attention(0)
            for q in range(4):
                lo(WO_A0 + q)
            residual_and_gain(1, WO_A0, 8, T)
            mlp(0, MLP_A0, None, True)
            lo(QD0 + 1)
            variance(2, 5)
            link(v.memset(zr[:], 0.0))
            dve.wait_ge(rstd_ready, 3)
            for zi in range(10):
                t = zi % 5
                r = TILE_ROWS[t]
                bank = 6 + zi % 2
                if t < NT:
                    dve.wait_ge(z_ps, zi - zi // 5 + 1)
                else:
                    dve.wait_ge(half_used, QD0 if zi < 5 else KVU0)
                if zi < 5:
                    v.tensor_scalar(zc[0:r, t, :], ps[0:r, bank, 0:KVR], rst[0:r, t:t + 1], None,
                                    ALU.mult).then_inc(z_evac, 1)
                    v.tensor_scalar(zr[0:r, t, :], ps[0:r, bank, KVR:KVR + ROPE], rst[0:r, t:t + 1], None,
                                    ALU.mult).then_inc(z_evac, 1)
                else:
                    v.tensor_scalar(zq[0:r, t, :], ps[0:r, bank, 0:QR], rst[0:r, t:t + 1], None,
                                    ALU.mult).then_inc(z_evac, 1)
                if zi == 4:
                    dve.wait_ge(z_sq, 5)
                    v.tensor_scalar(ss[:, 0, :], ss[:, 0, :], 1.0 / KVR, EPS, ALU.mult, ALU.add).then_inc(zv_ready, 1)
                    dve.wait_ge(zr_ready, 1)
                    dve.wait_ge(lat_in, 32)
                    for tt in range(5):
                        rr = TILE_ROWS[tt]
                        v.scalar_tensor_tensor(zc[0:rr, tt, :], zc[0:rr, tt, :], rc[0:rr, 0, tt:tt + 1],
                                               gckv[0:rr, :], ALU.mult, ALU.mult).then_inc(z_norm, 1)
                    lo(KVU0)
            lo(KVU0 + 1)
            dve.wait_ge(z_sq, 10)
            v.tensor_scalar(ss[:, 1, :], ss[:, 1, :], 1.0 / QR, EPS, ALU.mult, ALU.add).then_inc(zv_ready, 1)
            for f in range(2):
                dve.wait_ge(zT_hi, f + 1)
                v.tensor_tensor(ckvTl[:, f, :], pf[:, 1024 * f:1024 * f + KEYS], ckvTh[:, f, :].bitcast(F32),
                                ALU.subtract).then_inc(zT_lo, 1)
            dve.wait_ge(zr_ready, 2)
            dve.wait_ge(rope_in, 32)
            for t in range(5):
                r = TILE_ROWS[t]
                v.scalar_tensor_tensor(zq[0:r, t, :], zq[0:r, t, :], rc[0:r, 1, t:t + 1], gq[0:r, :],
                                       ALU.mult, ALU.mult).then_inc(z_norm, 1)
            cos = cst[:, C_COS:C_COS + 80].rearrange("p (t c) -> p t c", c=16)
            sin = cst[:, C_SIN:C_SIN + 80].rearrange("p (t c) -> p t c", c=16)
            x1, x2 = zr[:, :, 0:16], zr[:, :, 16:32]
            for i, (a, b) in enumerate(((x1, cos), (x2, sin), (x2, cos), (x1, sin))):
                v.tensor_tensor(krt[:, i, :, :], a, b, ALU.mult).then_inc(kr_chain, 1)
            dve.wait_ge(kr_chain, 4)
            v.tensor_tensor(krn[:, 0:5, 0:16], krt[:, 0, :, :], krt[:, 1, :, :], ALU.subtract)
            v.tensor_tensor(krn[:, 0:5, 16:32], krt[:, 2, :, :], krt[:, 3, :, :], ALU.add).then_inc(kr_ready, 1)
            lo(QU0)
            lo(QU0 + 1)
            for f in range(3):
                dve.wait_ge(zT_hi, f + 3)
                c = 2048 + 1024 * (f % 2)
                v.tensor_tensor(cqTl[:, f, :], pf[:, c:c + T], cqTh[:, f, :].bitcast(F32),
                                ALU.subtract).then_inc(zT_lo, 1)
            lo(QU0 + 2)
            lo(QU0 + 3)
            attention(1)
            for q in range(4):
                lo(WO_B0 + q)
            residual_and_gain(3, WO_B0, 32, T1)
            mlp(1, MLP_B0, 40, False)
            variance(4, 6)

        @block.tensor
        def _(pe):
            te = nc.tensor

            def mm(out, a, b, start, stop):
                return te.matmul(out, a, b, start=start, stop=stop)

            def token_stats(b, bank):
                pe.wait_ge(sacc_ready, 7 * (b + 1))
                for t in range(5):
                    i = mm(ps[:, bank, t:t + 1], sacc[:, P * t:P * t + P], ones[:, 0:1], True, True)
                i.then_inc(stat_ps, 1)

            def spread_stats(b):
                pe.wait_ge(sacc_ready, 7 * (b + 1))
                mm(ps[:, 6, :], ones, sacc[:, 0:512], True, True)
                mm(ps[:, 7, 0:T - 512], ones, sacc[:, 512:T], True, True).then_inc(stat_ps, 1)

            def tokens_product(out, xs, ws, k_n, rows, cols, gates=None, mid=None):
                (ah, al), (bh, bl) = xs, ws
                for k in range(k_n):
                    if gates:
                        gates(k)
                    mm(out, ah(k), bh(k), k == 0, False)
                    mm(out, ah(k), bl(k), False, False)
                    i = mm(out, al(k), bh(k), False, k == k_n - 1)
                    if mid and k == mid[0]:
                        i.then_inc(mid[1], 1)
                return i

            def x_tile(t):
                c = slice(P * t, P * t + TILE_ROWS[t])
                return (lambda k: xgh[:, k, c]), (lambda k: xgl[:, k, c])

            def split_halves(tensor, j, cols):
                return lambda k: view(tensor, j + k // 4)[:, k % 4, cols]

            pe.wait_ge(cst_in, 16)
            pe.wait_ge(gain_in, 96)
            te.transpose(ps[:, 6, 0:48], gn[:], ident[0:48, 0:48]).then_inc(gT_ps, 1)
            pe.wait_ge(x_in, 96)
            for k in range(KD):
                if k == 3:
                    pe.wait_ge(gT_ready, 1)
                if k >= 4:
                    pe.wait_ge(x_ready, k - 3)
                for t in range(5):
                    r = TILE_ROWS[t]
                    c = 1024 * (k % 4) + P * t
                    i = te.transpose(pf[:, c:c + r], xn[0:r, t, P * k:P * k + P], ident[0:r, 0:r])
                i.then_inc(xT_ps, 1)
            pe.wait_ge(x_ready, KD)
            token_stats(0, 6)
            pe.wait_ge(wf_lo, 1)
            pe.wait_ge(gl_ready, KD)
            for t in range(5):
                i = tokens_product(ps[0:TILE_ROWS[t], 7, 16 * t:16 * t + 16], x_tile(t),
                                   ((lambda k: wfh[:, k, :]), (lambda k: wfl[:, k, :])), KD, TILE_ROWS[t], 16)
            i.then_inc(f_ps, 1)

            for b in range(6):
                for t in range(5):
                    n = 5 * b + t
                    if n >= 4:
                        pe.wait_ge(blk_evac, n - 3)
                    out = ps[0:TILE_ROWS[t], n % 4, :]

                    def gates(k):
                        if t == 0 and k % 4 == 0:
                            pe.wait_ge(lo_done, 2 * b + 1 + k // 4)
                    i = tokens_product(out, x_tile(t), (split_halves(wh, 2 * b, slice(0, 512)),
                                                        split_halves(wl, 2 * b, slice(0, 512))),
                                       KD, TILE_ROWS[t], 512, gates, (3, half_used) if t == NT else None)
                    i.then_inc(blk_ps if t < NT else half_used, 1)
                if b == 0:
                    pe.wait_ge(f_chain, F_CHAIN)
                    pe.wait_ge(small_in, 64)
                    U, M4 = cst[:, C_U:C_U + P], cst[0:TX, C_META:C_META + P]
                    tri, sam = cst[0:TX, C_TRI:C_TRI + TX], cst[:, C_SAM:C_SAM + TX]
                    sums = [(t, P, [(M4, lg[0:TX, NT, :])] + [(ones, lg[:, i, :]) for i in range(t)] + [(U, lg[:, t, :])])
                            for t in range(NT)]
                    sums += [(NT, TX, [(sam, lg[:, 5, :]), (sam, lg[:, 6, :]), (tri, lg[0:TX, NT, :])]),
                             (5, P, [(U, lg[:, 5, :])]), (6, P, [(ones, lg[:, 5, :]), (U, lg[:, 6, :])])]
                    for t, r, terms in sums:
                        for n, (a, l) in enumerate(terms):
                            i = mm(ps[0:r, 5, 16 * t:16 * t + 16], a, l, n == 0, n == len(terms) - 1)
                    i.then_inc(F_ps, 1)

            def attention(layer):
                U0, G0, H0 = 5 * HEADS * layer, 9 * HEADS * layer, HEADS * layer
                R = R_FOX if layer == 0 else R_MLA
                m0 = MD * layer

                def scores(h, c, u):
                    k0, n = unit_keys(u)
                    rows = P if u < NT else TX
                    q0 = P * u
                    base_col = S_COL[u]
                    before = [-1, -1, 0, 2, 3][u] + U0
                    if not (isinstance(h, int) and h * 5 + before < 1):
                        pe.wait_ge(exp_done, h * 5 + before)
                    a_h, a_l = qh[0:R, c, q0:q0 + rows], ql[0:R, c, q0:q0 + rows]
                    mk0 = n - P if u < NT else 0
                    mcol = m0 if u < NT else m0 + P
                    i = None
                    for c0 in range(0, n, 512):
                        c1 = min(c0 + 512, n)
                        out = pf[0:rows, base_col + c0:base_col + c1]
                        kk = slice(k0 + c0, k0 + c1)
                        mm(out, a_h, kh[0:R, c, kk], True, False)
                        d0, d1 = max(c0, mk0), c1
                        te.matmul(pf[0:rows, base_col + d0:base_col + d1], idr[:, 0:rows],
                                  mask[:, mcol + d0 - mk0:mcol + d1 - mk0], start=False, stop=False,
                                  skip_group_check=True)
                        mm(out, a_h, kl[0:R, c, kk], False, False)
                        i = mm(out, a_l, kh[0:R, c, kk], False, True)
                    i.then_inc(s_ps, 1)

                def free_bank(h, q):
                    if not (isinstance(h, int) and group_at(h, q) + G0 < 3):
                        pe.wait_ge(g_lo, group_at(h, q) + (G0 - 2))

                def p_turn(h, c, q):
                    u, part = P_PARTS[q]
                    free_bank(h, q)
                    pe.wait_ge(p_ready, h * 5 + (U0 + u - 4))
                    bank = 3 + q % 3
                    if u == NT:
                        o = P_OFF[NT]
                        for j in range(3):
                            i = te.transpose(ps[:, bank, TX * j:TX * j + TX], prob[0:TX, 1 - c, o + P * j:o + P * j + P],
                                             ident[0:TX, 0:TX])
                    else:
                        n = min(u + 2, 4) if part == 0 else 1
                        for j in range(n):
                            b = j if part == 0 else 4
                            o = P_OFF[u] + (0 if b == 0 else TX + P * (b - 1))
                            i = te.transpose(ps[:, bank, P * j:P * j + P], prob[:, 1 - c, o:o + P], ident)
                    i.then_inc(g_ps, 1)

                def prep(h, q, nxt_c, g):
                    nq, nk = natq[layer], natk[layer]
                    rk = R_FOX if layer == 0 else 2 * HD
                    kc = nxt_c * R_FOX if layer == 0 else 2 * HD * nxt_c
                    qc = nxt_c * R
                    free_bank(h, q)
                    bank = 3 + q % 3
                    if g == 0:
                        for t in range(NT):
                            i = te.transpose(ps[0:R, bank, P * t:P * t + P], nq[:, t, qc:qc + R], ident)
                    elif g == 1:
                        for t in range(2):
                            te.transpose(ps[0:rk, bank, P * t:P * t + P], nk[:, 5 + t, kc:kc + rk], ident)
                        te.transpose(ps[0:rk, bank, 256:336], nk[0:TX, NT, kc:kc + rk], ident[0:TX, 0:TX])
                        i = te.transpose(ps[0:R, bank, 336:416], nq[0:TX, NT, qc:qc + R], ident[0:TX, 0:TX])
                    else:
                        for t in range(NT):
                            i = te.transpose(ps[0:rk, bank, P * t:P * t + P], nk[:, t, kc:kc + rk], ident)
                    i.then_inc(g_ps, 1)

                def weighted_v(prev, groups, pair):
                    pe.wait_ge(g_lo, groups)
                    pe.wait_ge(v_split, pair + (PAIRS * layer + 1))
                    if not (isinstance(prev, int) and prev + H0 < 1):
                        pe.wait_ge(o_lo, prev + H0)
                    ptv_h = pth[:, 0:2560].rearrange("p (b q) -> p b q", q=512)
                    ptv_l = ptl[:, 0:2560].rearrange("p (b q) -> p b q", q=512)
                    for b in (0, 2, 3, 4, 1):
                        t, rows, q0 = (NT, TX, 0) if b == 0 else (b - 1, P, P * (b - 1))
                        out = pf[:, 3072 + q0:3072 + SEQ]
                        pr_h, pr_l = ptv_h[0:rows, b, q0:SEQ], ptv_l[0:rows, b, q0:SEQ]
                        te.matmul(out, vh[0:rows, t, :], pr_h, start=(b == 0), stop=False, skip_group_check=True)
                        te.matmul(out, vh[0:rows, t, :], pr_l, start=False, stop=False, skip_group_check=True)
                        te.matmul(out, vl[0:rows, t, :], pr_h, start=False, stop=(b == 1), skip_group_check=True)
                    for b, (t, rows) in enumerate(((5, P), (6, P), (NT, TX))):
                        out = ps[:, 7, 0:TX]
                        c0 = 2560 + TX * b
                        te.matmul(out, vh[0:rows, t, :], pth[0:rows, c0:c0 + TX], start=(b == 0), stop=False)
                        te.matmul(out, vh[0:rows, t, :], ptl[0:rows, c0:c0 + TX], start=False, stop=False)
                        i = te.matmul(out, vl[0:rows, t, :], pth[0:rows, c0:c0 + TX], start=False, stop=(b == 2))
                    i.then_inc(av_done, 1)

                def step(h, c, pair, first=False, last=False):
                    for u in range(5):
                        if not first:
                            p_turn(h, c, u if u < 4 else 5)
                            if u == 3:
                                p_turn(h, c, 4)
                        if u == 0:
                            pe.wait_ge(g_lo, h * 9 + (G0 if first else G0 - 3) + (3 if first else 0))
                        scores(h, c, u)
                    if not last:
                        if c == 1:
                            pe.wait_ge(nat_qk, (pair + 1) * 80 + (80 + 80 * PAIRS * layer))
                        for g in range(3):
                            prep(h, 6 + g, 1 - c, g)
                    if not first:
                        weighted_v(h - 1, h * 9 + (G0 + 3), pair if c else pair - 1)

                if layer == 0:
                    pe.wait_ge(F_ready, 1)
                    pe.wait_ge(blk_evac, 30)
                else:
                    pe.wait_ge(lat_evac, 48)
                    pe.wait_ge(kr_lo, 1)
                pe.wait_ge(masks_ready, 2)
                pe.wait_ge(nat_qk, 80 + 80 * PAIRS * layer)
                for g in range(3):
                    prep(-1, 12 + g, 0, g)
                step(0, 0, 0, first=True)
                step(1, 1, 0)
                with pe.Fori(1, PAIRS - 1) as i:
                    step(2 * i, 0, i)
                    step(2 * i + 1, 1, i)
                step(HEADS - 2, 0, PAIRS - 1)
                step(HEADS - 1, 1, PAIRS - 1, last=True)
                for q in range(6):
                    p_turn(HEADS, 0, q)
                weighted_v(HEADS - 1, HEADS * 9 + G0, PAIRS - 1)

            def out_projection(layer, j0):
                n = T if layer == 0 else T1
                b = 2 * layer + 1
                pe.wait_ge(o_lo, HEADS * (layer + 1))
                pe.wait_ge(exp_done, 5 * HEADS * (layer + 1))
                for m in range(KD):
                    j = j0 + m // 2
                    pe.wait_ge(lo_done, j + 1)
                    if m >= 2:
                        pe.wait_ge(x_ready, KD * b + m - 1)
                    c = slice(P * (m % 2), P * (m % 2) + P)
                    i = transposed(m % 2, view(wh, j), view(wl, j), c, oh, ol, KD, n)
                    i.then_inc(half_used if m % 2 else wo_ps, 1)

            def transposed(pair, w_h, w_l, c, x_h, x_l, k_n, n, gate=None):
                for k in range(k_n):
                    if gate:
                        gate(k)
                    for p, (w, x) in enumerate(((w_h, x_h), (w_h, x_l), (w_l, x_h))):
                        for t in range(2):
                            i = mm(ps[:, 2 * pair + t, 0:n // 2], w[:, k, c], x[:, k, t * (n // 2):(t + 1) * (n // 2)],
                                   k == 0 and p == 0, k == k_n - 1 and p == 2)
                return i

            def mlp(layer, j0):
                n = T if layer == 0 else T1
                b = 2 * layer + 1

                def up(c, j, it=0, first=False):
                    for m in range(2):
                        if m == 0:
                            pe.wait_ge(lo_done, it * 4 + (j + 1))
                        if not first:
                            pe.wait_ge(u_lo, c * 2 + (m - 1 + 2 * NCH * layer))
                        cols = slice(P * m, P * m + P)
                        i = transposed(m, mlp_views(wh, j)[0], mlp_views(wl, j)[0], cols, xgh, xgl, KD, n,
                                       (lambda k: pe.wait_ge(gl_ready, KD * b + k + 1)) if first and m == 0 else None)
                        i.then_inc(half_used if m else u_ps, 1)

                def down(c, j, par_c, it=0):
                    pe.wait_ge(lo_done, it * 4 + (j + 1))
                    pe.wait_ge(u_lo, c * 2 + (2 + 2 * NCH * layer))
                    for m in range(KD):
                        pe.wait_ge(acc_done, c * KD + (m + 7 + ACC_N * layer))
                        cols = slice(P * m, P * m + P)
                        i = transposed(2 + m % 2, mlp_views(wh, j)[1], mlp_views(wl, j)[1], cols,
                                       hh[:, par_c], hl[:, par_c], 2, n)
                        i.then_inc(half_used if m == KD - 1 else d_ps, 1)

                pe.wait_ge(x_ready, KD * b + KD - 1)
                up(0, j0, first=True)
                spread_stats(b)
                pe.wait_ge(r2T_ready, layer + 1)
                with pe.Fori(0, NCH // 2 - 1) as i:
                    for q in range(2):
                        up(2 * i + q + 1, j0 + 2 * q + 1, i)
                        down(2 * i + q, j0 + 2 * q + 2, q, i)
                up(NCH - 1, j0 + 29)
                down(NCH - 2, j0 + 30, 0)
                down(NCH - 1, j0 + 31, 1)

            attention(0)
            out_projection(0, WO_A0)
            mlp(0, MLP_A0)

            pe.wait_ge(x_ready, 3 * KD)
            token_stats(2, 5)
            for zi in range(10):
                t, r = zi % 5, TILE_ROWS[zi % 5]
                j, w = (KVD0, KVR + ROPE) if zi < 5 else (QD0, QR)
                if zi >= 2:
                    pe.wait_ge(z_evac, 2 * (zi - 1) if zi - 2 < 5 else zi + 4)

                def gates(k):
                    if t == 0 and k % 4 == 0:
                        pe.wait_ge(lo_done, j + 1 + k // 4)
                    if zi == 0:
                        pe.wait_ge(gl_ready, 2 * KD + k + 1)
                i = tokens_product(ps[0:r, 6 + zi % 2, 0:w], x_tile(t),
                                   (split_halves(wh, j, slice(0, w)), split_halves(wl, j, slice(0, w))),
                                   KD, r, w, gates, (3, half_used) if t == NT else None)
                i.then_inc(z_ps if t < NT else half_used, 1)
            pe.wait_ge(z_norm, 5)
            pe.wait_ge(lat_in, 32)
            pe.wait_ge(rope_in, 32)
            for f in range(2):
                for t in range(7):
                    r = TX if t == NT else P
                    c = 1024 * f + (P * t if t <= NT else T + P * (t - 5))
                    i = te.transpose(pf[:, c:c + r], zc[0:r, t, P * f:P * f + P], ident[0:r, 0:r])
                i.then_inc(zT_ps, 1)
            pe.wait_ge(zT_lo, 2)
            for n in range(28):
                t, blk = (n % 14) // 2, n % 2
                r = TX if t == NT else P
                c0 = P * t if t <= NT else T + P * (t - 5)
                j = KVU0 + n // 14
                if n % 14 == 0:
                    pe.wait_ge(lo_done, j + 1)
                if n >= 4:
                    pe.wait_ge(lat_evac, n - 3)
                i = tokens_product(ps[0:r, n % 4, :], ((lambda k: ckvTh[:, k, c0:c0 + r]), (lambda k: ckvTl[:, k, c0:c0 + r])),
                                   ((lambda k: view(wh, j)[:, k, 512 * blk:512 * blk + 512]),
                                    (lambda k: view(wl, j)[:, k, 512 * blk:512 * blk + 512])), 2, r, 512)
                i.then_inc(half_used if n % 14 == 13 else lat_ps, 1)
            pe.wait_ge(z_norm, 10)
            pe.wait_ge(var_ready, 2)
            for f in range(3):
                if f == 2:
                    pe.wait_ge(zT_lo, 3)
                for t in range(5):
                    r = TILE_ROWS[t]
                    c = 2048 + 1024 * (f % 2) + P * t
                    i = te.transpose(pf[:, c:c + r], zq[0:r, t, P * f:P * f + P], ident[0:r, 0:r])
                i.then_inc(zT_ps, 1)
            pe.wait_ge(zT_lo, 5)
            for n in range(20):
                t, r = n % 5, TILE_ROWS[n % 5]
                j = QU0 + n // 5
                c = slice(P * t, P * t + r)
                if t == 0:
                    pe.wait_ge(lo_done, j + 1)
                pe.wait_ge(lat_evac, 28 + n - 3)
                i = tokens_product(ps[0:r, n % 4, 0:384], ((lambda k: cqTh[:, k, c]), (lambda k: cqTl[:, k, c])),
                                   ((lambda k: view(wh, j)[:, k, :]), (lambda k: view(wl, j)[:, k, :])), 3, r, 384)
                i.then_inc(half_used if t == NT else lat_ps, 1)
            pe.wait_ge(kr_ready, 1)
            for t in range(NT):
                te.transpose(pf[0:ROPE, 3072 + P * t:3072 + P * t + P], krn[:, t, :], ident)
            for t in range(2):
                te.transpose(pf[0:ROPE, 3584 + P * t:3584 + P * t + P], krn[:, 5 + t, :], ident)
            te.transpose(pf[0:ROPE, 3840:3920], krn[0:TX, NT, :], ident[0:TX, 0:TX]).then_inc(kr_ps, 1)

            attention(1)
            out_projection(1, WO_B0)
            mlp(1, MLP_B0)
            pe.wait_ge(x_ready, 5 * KD)
            token_stats(4, 6)
            pe.wait_ge(y_scaled, KD)
            for t in range(5):
                r = P if t < NT else SAM
                if t >= 2:
                    pe.wait_ge(y_evac, t - 1)
                for k in range(KD):
                    c = 1024 * (t % 2) + P * k
                    i = te.transpose(pf[0:r, c:c + P], yT[:, k, P * t:P * t + r], ident)
                i.then_inc(y_ps, 1)


def constants():
    import numpy as np
    c = np.zeros((P, C_N), np.float32)
    c[:, C_ID:C_ID + P] = np.eye(P)
    c[:, C_U:C_U + P] = np.triu(np.ones((P, P)))
    c[:, C_ONE:C_ONE + P] = 1
    c[SAM:TX, C_META:C_META + P] = 1
    c[0:SAM, C_TRI:C_TRI + SAM] = np.triu(np.ones((SAM, SAM)))
    c[SAM:TX, C_TRI + SAM:C_TRI + TX] = np.triu(np.ones((META, META)))
    c[:, C_SAM:C_SAM + SAM] = 1
    pos = np.zeros((5, P), np.float32)
    for t in range(NT):
        pos[t] = META + P * t + np.arange(P)
    pos[NT, 0:SAM] = PAST + np.arange(SAM)
    pos[NT, SAM:TX] = np.arange(META)
    half = ROPE // 2
    inv = (np.float32(1.0) / np.power(np.float32(10000.0), np.arange(half, dtype=np.float32) * np.float32(2.0 / ROPE))).astype(np.float32)
    ang = (pos[:, :, None] * inv[None, None, :]).astype(np.float32)
    c[:, C_COS:C_COS + 80] = np.cos(ang).transpose(1, 0, 2).reshape(P, 80)
    c[:, C_SIN:C_SIN + 80] = np.sin(ang).transpose(1, 0, 2).reshape(P, 80)
    NEG = -1e30
    m = np.zeros((P, M_N), np.float32)
    r = np.arange(P)
    for layer in range(2):
        d = m[:, MD * layer:MD * layer + P]
        d[:] = np.where(r[None, :] <= r[:, None], 0, NEG) if layer == 0 else np.where(r[None, :] // 64 <= r[:, None] // 64, 0, NEG)
        e = m[:, MD * layer + P:MD * layer + MD]
        rs, rm = np.arange(SAM), np.arange(META)
        e[0:SAM, PAST + SAM:] = NEG
        e[SAM:TX, 0:PAST + SAM] = NEG
        if layer == 0:
            e[0:SAM, PAST:PAST + SAM] = np.where(rs[None, :] <= rs[:, None], 0, NEG)
            e[SAM:TX, PAST + SAM:] = np.where(rm[None, :] <= rm[:, None], 0, NEG)
    return c, m


_INS = [("x_prompt", "x_prompt", (SEQ, D)), ("x_sample", "x_sample", (SAM, D)), ("meta_tokens", "meta_tokens", (META, D)),
        ("cache_k", "cache_fox_k", (PAST, D)), ("cache_v", "cache_fox_v", (PAST, D)),
        ("cache_logf", "cache_fox_logf", (PAST, HEADS)), ("cache_ckv", "cache_mla_ckv", (PAST, KVR)),
        ("cache_kr", "cache_mla_krope", (PAST, ROPE)), ("norm_mix", "norm_mix", (2, D)), ("norm_ffn", "norm_ffn", (2, D)),
        ("w_in_a", "w_in_a", (1, D, 3 * D + HEADS)), ("b_f", "b_f", (HEADS,)), ("w_o_a", "w_o_a", (1, D, D)),
        ("kv_norm", "kv_norm", (D,)), ("w_kv_down", "w_kv_down", (D, KVR + ROPE)), ("ckv_norm", "ckv_norm", (KVR,)),
        ("w_kv_up", "w_kv_up", (KVR, HEADS * 2 * HD)), ("w_q_down", "w_q_down", (1, D, QR)), ("q_norm", "q_norm", (QR,)),
        ("w_q_up", "w_q_up", (1, QR, HEADS * R_MLA)), ("w_o_b", "w_o_b", (1, D, D)), ("w_up", "w_up", (2, D, DFF)),
        ("w_down", "w_down", (2, DFF, D)), ("final_norm", "final_norm", (D,))]
_OUTS = [("y_p", (SEQ, D), (1, SEQ, D)), ("y_s", (SAM, D), (1, SAM, D)),
         ("o_k_p", (META + SEQ, D), (1, 1, META + SEQ, HEADS, HD)), ("o_v_p", (META + SEQ, D), (1, 1, META + SEQ, HEADS, HD)),
         ("o_lf_p", (META + SEQ, HEADS), (1, 1, META + SEQ, HEADS)), ("o_ckv_p", (META + SEQ, KVR), (1, META + SEQ, KVR)),
         ("o_kr_p", (META + SEQ, ROPE), (1, META + SEQ, ROPE)),
         ("o_k_s", (SAM, D), (1, 1, SAM, HEADS, HD)), ("o_v_s", (SAM, D), (1, 1, SAM, HEADS, HD)),
         ("o_lf_s", (SAM, HEADS), (1, 1, SAM, HEADS)), ("o_ckv_s", (SAM, KVR), (1, SAM, KVR)),
         ("o_kr_s", (SAM, ROPE), (1, SAM, ROPE))]


def kernel(**inputs):
    import numpy as np
    import concourse.bacc as bacc
    from concourse.bass_utils import run_bass_kernel_spmd

    nc = bacc.Bacc("TRN2", target_bir_lowering=False, num_devices=1)
    arrays, io = {}, {}
    for name, key, shape in _INS:
        a = np.ascontiguousarray(inputs[key]).reshape(shape)
        arrays[f"in_{name}"] = a
        io[name] = nc.dram_tensor(f"in_{name}", a.shape, mybir.dt.from_np(a.dtype), kind="ExternalInput").ap()
    for name, a in zip(("cst", "masks"), constants()):
        arrays[f"in_{name}"] = a
        io[name] = nc.dram_tensor(f"in_{name}", a.shape, F32, kind="ExternalInput").ap()
    for name, shape, _ in _OUTS:
        io[name] = nc.dram_tensor(f"out_{name}", shape, F32, kind="ExternalOutput").ap()
    build(nc, io)
    r = run_bass_kernel_spmd(nc, [arrays], core_ids=[0])
    return tuple(np.asarray(r.results[0][f"out_{name}"]).reshape(ret) for name, _, ret in _OUTS)
```

```python
from contextlib import ExitStack

import concourse.bass as bass
from concourse import mybir

F32 = mybir.dt.float32
F32R = mybir.dt.float32r
ALU = mybir.AluOpType
ACT = mybir.ActivationFunctionType
AX = mybir.AxisListType

P = 128
D = 1024
KD = D // P
SEQ, SAM, META, PAST = 512, 64, 16, 256
T = SEQ + SAM + META
TX = SAM + META
NT = SEQ // P
TH = T // 2
T1 = SEQ + SAM
KEYS = T + PAST
HEADS, HD = 16, 64
PAIRS = HEADS // 2
ROPE = 32
KVR, QR = D // 4, 3 * D // 8
DFF = 4 * D
CH = 256
NCH = DFF // CH
EPS = 1e-6
FOX_SCALE = HD ** -0.5
MLA_SCALE = (HD + ROPE) ** -0.5
HALF = 2048
R_FOX, R_MLA = HD + 2, HD + ROPE
TILE_ROWS = [P] * NT + [TX]

W_IN0, WO_A0, MLP_A0 = 0, 12, 16
KVD0, QD0, KVU0, QU0, WO_B0, MLP_B0, W_END = 48, 50, 52, 54, 58, 62, 94

C_ID, C_U, C_ONE, C_META, C_TRI, C_SAM, C_COS, C_SIN = 0, 128, 256, 384, 512, 592, 672, 752
C_N = 832
M_N = 2 * (P + META + SAM + PAST)
MD = P + META + SAM + PAST


def unit_keys(u):
    return (PAST + SAM, META + P * (u + 1)) if u < NT else (0, PAST + SAM + META)


ACC_N = KD * (NCH + 1)
F_CHAIN = 18
P_OFF = [0, 208, 544, 1008, 1600]
P_N = 1984


def build(nc, io):
    ctx = ExitStack()
    with ctx:
        base = 16512
        top = {"at": base}

        def region(nbytes):
            at = top["at"]
            top["at"] = at + (nbytes + 31) // 32 * 32
            assert top["at"] <= nc.sbuf_usable_end, top["at"]
            return at

        def at(name, shape, dt, offset):
            return nc.alloc_sbuf_tensor_at(name, shape, dt, offset=(offset + 31) // 32 * 32)

        def sb(name, shape, dt=F32):
            n = 4
            for s in shape[1:]:
                n *= s
            return at(name, shape, dt, region(n))

        R_RAW = region(4 * HALF * 4)
        R_W = region(8 * HALF * 4)
        R_G = region(2 * KD * T * 4)
        R_O = region(2 * KD * T * 4)
        raw = at("raw", [P, 4, HALF], F32, R_RAW)
        wh = at("wh", [P, 4, HALF], F32R, R_W)
        wl = at("wl", [P, 4, HALF], F32R, R_W + 4 * HALF * 4)
        xT = sb("xT", [P, KD, T])
        o = R_W
        pth = at("pth", [P, 2800], F32R, o); o += 11200
        ptl = at("ptl", [P, 2800], F32R, o); o += 11200
        qh = at("qh", [R_MLA, 2, T], F32R, o); o += 8 * T
        ql = at("ql", [R_MLA, 2, T], F32R, o); o += 8 * T
        kh = at("kh", [R_MLA, 2, KEYS], F32R, o); o += 8 * KEYS
        kl = at("kl", [R_MLA, 2, KEYS], F32R, o); o += 8 * KEYS
        prob = at("prob", [P, 2, P_N], F32, (o + 31) // 32 * 32)
        xgh = at("xgh", [P, KD, T], F32R, R_G)
        xgl = at("xgl", [P, KD, T], F32R, R_G + KD * T * 4)
        natq = [[at(f"natq0_{i}", [P, 5, 2 * R_FOX], F32, R_G + 2656 * i) for i in range(2)],
                [at(f"natq1_{i}", [P, 5, 2 * R_MLA], F32, R_G + 3840 * i) for i in range(2)]]
        natk = [[at(f"natk0_{i}", [P, 7, 2 * R_FOX], F32, R_G + 5312 + 3712 * i) for i in range(2)],
                [at(f"natk1_{i}", [P, 7, 4 * HD], F32, R_G + 9216 + 7168 * i) for i in range(2)]]
        natv0 = at("natv0", [P, 7, P], F32, R_G + 12736)
        vh = at("vh", [P, 2, 7, P], F32R, R_G + 23552)
        vl = at("vl", [P, 2, 7, P], F32R, R_G + 23552 + 7168)
        yT = at("yT", [P, KD, T1], F32, R_G)
        oh = at("oh", [P, PAIRS, T], F32R, R_O)
        ol = at("ol", [P, PAIRS, T], F32R, R_O + KD * T * 4)
        xn = at("xn", [P, 5, D], F32, R_O)
        ckn = at("ckn", [P, 2, D], F32, R_O + 20480)
        cka = at("cka", [P, 2, HEADS, R_FOX], F32, R_O + 28672)
        stg = at("stg", [P, 4, 8 * R_FOX], F32, R_O)
        acc = at("acc", [P, KD, T], F32, R_O)
        hh = at("hh", [P, 2, 2, T], F32R, R_O + 18944)
        hl = at("hl", [P, 2, 2, T], F32R, R_O + 18944 + 9472)
        ckvTh = at("ckvTh", [P, 2, KEYS], F32R, R_O)
        ckvTl = at("ckvTl", [P, 2, KEYS], F32R, R_O + 6784)
        cqTh = at("cqTh", [P, 3, T], F32R, R_O + 13568)
        cqTl = at("cqTl", [P, 3, T], F32R, R_O + 13568 + 7104)
        zc = at("zc", [P, 7, KVR], F32, R_O + 13568)
        zq = at("zq", [P, 5, QR], F32, R_O + 27776)
        gckv = at("gckv", [P, KVR], F32, R_O + 35456)
        stn = at("stn", [P, 4, 512], F32, R_G)
        rtmp = at("rtmp", [P, 4, 4, ROPE // 2], F32, R_G + 8192)
        yst = at("yst", [P, 2, D], F32, R_O)
        mraw = at("mraw", [P, M_N], F32, R_RAW)

        cst = sb("cst", [P, C_N])
        idr = sb("idr", [P, P], F32R)
        mask = sb("mask", [P, M_N], F32R)
        gn = at("gn", [48, P], F32, R_RAW + HALF * 4)
        gT = sb("gT", [P, 48])
        bfb = sb("bfb", [P, HEADS])
        gq = at("gq", [P, QR], F32, R_G + 24000)
        sq = sb("sq", [P, 2, T])
        sacc = sb("sacc", [P, 5 * P])
        small = region(4 * T)
        r2T = at("r2T", [P, T], F32, small)
        v5 = sb("v5", [P, 5])
        rst = sb("rst", [P, 5])
        rst8 = sb("rst8", [P, 5])
        ss = sb("ss", [P, 2, 5])
        rc = sb("rc", [P, 2, 5])
        mhalf = sb("mhalf", [P, 5])
        wf = at("wf", [P, KD, HEADS], F32, small)
        wfh = at("wfh", [P, KD, HEADS], F32R, small + 512)
        wfl = at("wfl", [P, KD, HEADS], F32R, small + 1024)
        lg = sb("lg", [P, 7, HEADS])
        FQ = at("FQ", [P, 5, HEADS, 2], F32, small + 1536)
        keys = region(4 * 7 * HEADS * 2)
        FK = at("FK", [P, 7, HEADS, 2], F32, keys)
        nmx = sb("nmx", [P, 5])
        sm = sb("sm", [P, 5])
        rs = sb("rs", [P, 5])
        krn = at("krn", [P, 7, ROPE], F32, R_G + 20000)
        zr = at("zr", [P, 5, ROPE], F32, keys)
        krt = at("krt", [P, 4, 5, ROPE // 2], F32, R_G + 21056)
        ft = sq[:, 0, 0:480].rearrange("p (a b) -> p a b", a=6)
        fT = sq[0:HEADS, 1, :]
        ident = cst[:, C_ID:C_ID + P]
        ones = cst[:, C_ONE:C_ONE + P]

        qscr = [nc.dram_tensor("q_fox", (T, HEADS * R_FOX), F32, kind="Internal").ap(),
                nc.dram_tensor("q_mla", (T, HEADS * R_MLA), F32, kind="Internal").ap()]
        kscr = [nc.dram_tensor("k_fox", (KEYS, HEADS * R_FOX), F32, kind="Internal").ap(),
                nc.dram_tensor("kv_mla", (KEYS, HEADS * 2 * HD), F32, kind="Internal").ap()]

        ps = ctx.enter_context(nc.psum_tensor("ps", [P, 8, 512], F32))
        pf = ps[:, :, :].rearrange("p b c -> p (b c)")

        def sem(name):
            return ctx.enter_context(nc.semaphore(name))

        cst_in, mask_in, x_in, small_in = sem("cst_in"), sem("mask_in"), sem("x_in"), sem("small_in")
        gain_in = sem("gain_in")
        raw_in = [sem(f"raw_in{i}") for i in range(4)]
        hi_done, lo_done, half_used = sem("hi_done"), sem("lo_done"), sem("half_used")
        masks_ready, setup_ready = sem("masks_ready"), sem("setup_ready")
        gT_ps, gT_ready = sem("gT_ps"), sem("gT_ready")
        fT_ps, fT_ready = sem("fT_ps"), sem("fT_ready")
        xT_ps, x_ready = sem("xT_ps"), sem("x_ready")
        sq_ready, gh_ready, gl_ready, sacc_ready = sem("sq_ready"), sem("gh_ready"), sem("gl_ready"), sem("sacc_ready")
        stat_ps, var_ready, rstd_ready, r2T_ready = sem("stat_ps"), sem("var_ready"), sem("rstd_ready"), sem("r2T_ready")
        wf_hi, wf_lo, f_ps, f_chain, f_exp, F_ps, F_ready = (sem(n) for n in (
            "wf_hi", "wf_lo", "f_ps", "f_chain", "f_exp", "F_ps", "F_ready"))
        blk_ps, blk_evac, aug_done = sem("blk_ps"), sem("blk_evac"), sem("aug_done")
        st_out = [sem(f"st_out{i}") for i in range(4)]
        cka_ready, cka_out, lg_out = sem("cka_ready"), sem("cka_out"), sem("lg_out")
        nat_qk, nat_v = [sem("nat_qk0"), sem("nat_qk1")], sem("nat_v")
        v_hi, v_split = sem("v_hi"), sem("v_split")
        s_ps, max_done, exp_done, recip_done, p_ready = (sem(n) for n in (
            "s_ps", "max_done", "exp_done", "recip_done", "p_ready"))
        p3_ready = sem("p3_ready")
        g_ps, g_hi, g_lo = sem("g_ps"), sem("g_hi"), sem("g_lo")
        av_done, o_hi, o_lo, p_zero = sem("av_done"), sem("o_hi"), sem("o_lo"), sem("p_zero")
        wo_ps = sem("wo_ps")
        u_ps, u_relu, u_sq, u_hi, u_lo = (sem(n) for n in ("u_ps", "u_relu", "u_sq", "u_hi", "u_lo"))
        d_ps, acc_done, acc_scaled, x_d = sem("d_ps"), sem("acc_done"), sem("acc_scaled"), sem("x_d")
        z_ps, z_evac, z_sq, zv_ready, zr_ready, z_norm = (sem(n) for n in (
            "z_ps", "z_evac", "z_sq", "zv_ready", "zr_ready", "z_norm"))
        zT_ps, zT_hi, zT_lo, z_out = sem("zT_ps"), sem("zT_hi"), sem("zT_lo"), sem("z_out")
        lat_in, rope_in = sem("lat_in"), sem("rope_in")
        kr_chain, kr_ready, kr_ps, kr_T, kr_lo, rope_mul = (sem(n) for n in (
            "kr_chain", "kr_ready", "kr_ps", "kr_T", "kr_lo", "rope_mul"))
        lat_ps, lat_evac, lat_rope = sem("lat_ps"), sem("lat_evac"), sem("lat_rope")
        y_scaled, y_ps, y_evac, y_out = sem("y_scaled"), sem("y_ps"), sem("y_evac"), sem("y_out")
        y_outs = [y_out, sem("y_out1")]

        def piece_shape(j):
            if j < WO_A0:
                return 4, 512
            if KVD0 <= j < QD0:
                return 4, KVR + ROPE
            if QD0 <= j < KVU0:
                return 4, QR
            if KVU0 <= j < QU0:
                return 2, 1024
            if QU0 <= j < WO_B0:
                return 3, 384
            return 8, 256

        def piece_gain(j, k):
            if KVD0 <= j < QD0:
                return gT[:, 16 + 4 * (j - KVD0) + k:17 + 4 * (j - KVD0) + k]
            if QD0 <= j < KVU0:
                return gT[:, 24 + 4 * (j - QD0) + k:25 + 4 * (j - QD0) + k]
            return None

        def view(t, j):
            r, c = piece_shape(j)
            return t[:, j % 4, 0:r * c].rearrange("p (k c) -> p k c", c=c)

        V_COL, K_COL, Q_COL = 2 * D, D, 0
        BLOCKS = [("v", 0), ("v", 1), ("k", 0), ("k", 1), ("q", 0), ("q", 1)]

        def stored(slot, upto):
            n = 0
            for i in range(slot, upto, 4):
                kind = BLOCKS[i // 5][0]
                n += {"v": 1, "k": 2, "q": 1}[kind] + (i % 5 == NT and kind != "q")
            return 16 * n

        def block_col(b):
            kind, half = BLOCKS[b]
            return {"v": V_COL, "k": K_COL, "q": Q_COL}[kind] + 512 * half

        w_in = io["w_in_a"][0]

        def piece_src(j):
            if j < WO_A0:
                b, hf = j // 2, j % 2
                c = block_col(b)
                return w_in[512 * hf:512 * hf + 512, c:c + 512].rearrange("(k p) n -> p k n", p=P)
            if j < MLP_A0:
                c = CH * (j - WO_A0)
                return io["w_o_a"][0][:, c:c + CH].rearrange("(k p) n -> p k n", p=P)
            if j < QD0:
                r = 512 * (j - KVD0)
                return io["w_kv_down"][r:r + 512, :].rearrange("(k p) n -> p k n", p=P)
            if j < KVU0:
                r = 512 * (j - QD0)
                return io["w_q_down"][0][r:r + 512, :].rearrange("(k p) n -> p k n", p=P)
            if j < QU0:
                c = 1024 * (j - KVU0)
                return io["w_kv_up"][:, c:c + 1024].rearrange("(k p) n -> p k n", p=P)
            if j < WO_B0:
                c = 384 * (j - QU0)
                return io["w_q_up"][0][:, c:c + 384].rearrange("(k p) n -> p k n", p=P)
            c = CH * (j - WO_B0)
            return io["w_o_b"][0][:, c:c + CH].rearrange("(k p) n -> p k n", p=P)

        def up_src(layer, c):
            return io["w_up"][layer].rearrange("(k p) n -> p k n", p=P)[:, :, bass.ds(c * CH, CH)]

        def down_src(layer, c):
            return io["w_down"][layer].rearrange("(c k p) n -> c p k n", p=P, k=2)[c]

        def wait_tile(eng, b, t):
            if t < NT:
                eng.wait_ge(blk_ps, 4 * b + t + 1)
            else:
                eng.wait_ge(half_used, 2 * b + 2)

        def wait_lat(eng, n):
            if n < 28:
                eng.wait_ge(half_used, KVU0 + 1 + n // 14) if n % 14 == 13 else eng.wait_ge(lat_ps, n - n // 14 + 1)
            else:
                m = n - 28
                eng.wait_ge(half_used, QU0 + 1 + m // 5) if m % 5 == 4 else eng.wait_ge(lat_ps, 26 + m - m // 5 + 1)

        def mlp_views(t, j):
            up = t[:, j % 4, :].rearrange("p (k c) -> p k c", c=CH)
            down = t[:, j % 4, :].rearrange("p (k c) -> p k c", c=D)
            return up, down

        def p_group(u, part):
            def copies(bank, q_, k_, pt):
                if u == NT:
                    return [(pt[:, 2560:2800], ps[:, bank, 0:240])]
                n = min(u + 2, 4) if part == 0 else 1
                b0 = 0 if part == 0 else 4
                dst = pt[:, 0:2560].rearrange("p (b q) -> p b q", q=512)[:, b0:b0 + n, P * u:P * u + P]
                return [(dst, ps[:, bank, 0:P * n].rearrange("p (b q) -> p b q", q=P))]
            return copies

        S_BANK = [0, 1, 2, 0, 2]
        Z_BANK = [6, 7, 4]

        def logits(u):
            rows, n, b = TILE_ROWS[u], unit_keys(u)[1], S_BANK[u]
            if u == NT - 1:
                return ps[0:rows, b:b + 2, 0:n // 2], lambda row: row.rearrange("p (a c) -> p a c", a=2)
            return ps[0:rows, b, 0:n], lambda row: row

        P_PARTS = [(0, 0), (1, 0), (2, 0), (3, 0), (3, 1), (NT, 0)]

        def place(h, what, k):
            if isinstance(h, int) and (h < 1 or h >= HEADS - 1):
                return k
            return [0, 2, 4, 6, 7, 8][k] if what == "p" else 2 * k + 1

        def group_at(h, q):
            if isinstance(h, int):
                return 3 * h + 3 + q if h < 1 else h * 9 + q - (6 if h == HEADS else 3)
            return h * 9 + (q - 3)

        def p_split(h, k):
            return group_at(h, place(h, "p", k)) + 1

        def qk_split(h):
            return group_at(h - 1, place(h - 1, "q", 2)) + 1 if isinstance(h, int) else h * 9 - 6

        def prep_group(layer, q, slot):
            rq = R_FOX if layer == 0 else R_MLA
            rk = R_FOX if layer == 0 else HD

            def copies(bank, q_, k_, pt):
                if q == 0:
                    return [(q_[0:rq, slot, 0:SEQ], ps[0:rq, bank, 0:SEQ])]
                if q == 1:
                    return [(k_[0:rk, slot, 0:336], ps[0:rk, bank, 0:336]),
                            (q_[0:rq, slot, SEQ:T], ps[0:rq, bank, 336:416])]
                return [(k_[0:rk, slot, 336:KEYS], ps[0:rk, bank, 0:SEQ])]
            return copies

        okp, ovp = io["o_k_p"], io["o_v_p"]
        oks, ovs = io["o_k_s"], io["o_v_s"]

        def two_banks(pair, n):
            return ps[:, 2 * pair:2 * pair + 2, 0:n // 2]

        def halves(ap):
            return ap.rearrange("p (a b) -> p a b", a=2)

        block = ctx.enter_context(nc.Block())

        @block.sync
        def _(sp):
            def load(j):
                if j >= 4:
                    sp.wait_ge(lo_done, j - 3)
                r, c = piece_shape(j)
                sp.dma_start(view(raw, j), piece_src(j)).then_inc(raw_in[j % 4], 16)

            x = io["x_prompt"]
            sp.dma_start(cst[:], io["cst"]).then_inc(cst_in, 16)
            sp.dma_start(mraw[:], io["masks"]).then_inc(mask_in, 16)
            for i, g in enumerate((io["norm_mix"][0], io["norm_ffn"][0], io["kv_norm"], io["norm_mix"][1],
                                   io["norm_ffn"][1], io["final_norm"])):
                sp.dma_start(gn[8 * i:8 * i + 8, :], g.rearrange("(k p) -> k p", p=P)).then_inc(gain_in, 16)
            for t in range(NT):
                sp.dma_start(xn[:, t, :], x[P * t:P * t + P, :]).then_inc(x_in, 16)
            sp.dma_start(xn[0:SAM, NT, :], io["x_sample"]).then_inc(x_in, 16)
            sp.dma_start(xn[SAM:TX, NT, :], io["meta_tokens"]).then_inc(x_in, 16)
            sp.wait_ge(masks_ready, 1)
            load(0)
            sp.wait_ge(gT_ps, 1)
            load(1)
            sp.dma_start(wf[:], w_in[:, 3 * D:3 * D + HEADS].rearrange("(k p) n -> p k n", p=P)).then_inc(small_in, 16)
            sp.dma_start(bfb[:], io["b_f"].partition_broadcast(P)).then_inc(small_in, 16)
            sp.dma_start(lg[:, 5:7, :], io["cache_logf"].rearrange("(t p) h -> p t h", p=P)).then_inc(small_in, 16)
            for j in range(2, 4):
                load(j)
            sp.dma_start(ckn[:], io["cache_k"].rearrange("(t p) n -> p t n", p=P)).then_inc(small_in, 16)

            for b, (kind, hf) in enumerate(BLOCKS):
                for j in (2 * b + 4, 2 * b + 5):
                    load(j)
                if b == 2:
                    sp.wait_ge(F_ready, 1)
                    lgo = io["o_lf_p"]
                    sp.dma_start(lgo[META:, :].rearrange("(t p) h -> p t h", p=P), lg[:, 0:NT, :]).then_inc(lg_out, 16)
                    sp.dma_start(lgo[0:META, :], lg[SAM:TX, NT, :]).then_inc(lg_out, 16)
                    sp.dma_start(io["o_lf_s"], lg[0:SAM, NT, :]).then_inc(lg_out, 16)
                    sp.wait_ge(cka_ready, 2)
                    sp.dma_start(kscr[0][T:, :].rearrange("(t p) n -> p t n", p=P),
                                 cka[:, :, :, :].rearrange("p t h r -> p t (h r)")).then_inc(cka_out, 16)
                for t in range(5):
                    n = 5 * b + t
                    sp.wait_ge(blk_evac, n + 1)
                    if kind != "v":
                        sp.wait_ge(aug_done, n - 9)
                    done = st_out[n % 4]
                    cols = slice(512 * hf, 512 * hf + 512)
                    rows = slice(P * t, P * t + TILE_ROWS[t])
                    if kind == "v":
                        src = stg[:, n % 4, 0:512]
                        op, os_ = ovp, ovs
                    else:
                        scr = (kscr if kind == "k" else qscr)[0]
                        sp.dma_start(scr[rows, 528 * hf:528 * hf + 528],
                                     stg[0:TILE_ROWS[t], n % 4, :]).then_inc(done, 16)
                        if kind == "q":
                            continue
                        src = stg[:, n % 4, :].rearrange("p (h r) -> p h r", r=R_FOX)[:, :, 0:HD]
                        op, os_ = okp, oks

                    def dst(ap):
                        return ap if kind == "v" else ap.rearrange("p (h r) -> p h r", r=HD)
                    if t < NT:
                        sp.dma_start(dst(op[META + P * t:META + P * t + P, cols]), src).then_inc(done, 16)
                    else:
                        sp.dma_start(dst(os_[:, cols]), src[0:SAM]).then_inc(done, 16)
                        sp.dma_start(dst(op[0:META, cols]), src[SAM:TX]).then_inc(done, 16)

            def fox_qk(j, slot):
                c = bass.ds(j * (2 * R_FOX), 2 * R_FOX)
                for scr, nat in ((qscr[0], natq[0][slot]), (kscr[0], natk[0][slot])):
                    sp.dma_start(nat[:, 0:NT, :], scr[0:SEQ, c].rearrange("(t p) n -> p t n", p=P)).then_inc(nat_qk[slot], 16)
                    sp.dma_start(nat[0:TX, NT, :], scr[SEQ:T, c]).then_inc(nat_qk[slot], 16)
                sp.dma_start(natk[0][slot][:, 5:7, :],
                             kscr[0][T:, c].rearrange("(t p) n -> p t n", p=P)).then_inc(nat_qk[slot], 16)

            def fox_v(j):
                c = bass.ds(j * P, P)
                sp.dma_start(natv0[:, 0:NT, :], ovp[META:, c].rearrange("(t p) n -> p t n", p=P)).then_inc(nat_v, 16)
                sp.dma_start(natv0[0:SAM, NT, :], ovs[:, c]).then_inc(nat_v, 16)
                sp.dma_start(natv0[SAM:TX, NT, :], ovp[0:META, c]).then_inc(nat_v, 16)
                sp.dma_start(natv0[:, 5:7, :], io["cache_v"][:, c].rearrange("(t p) n -> p t n", p=P)).then_inc(nat_v, 16)

            def mla_kv(j, slot):
                c = bass.ds(j * (4 * HD), 4 * HD)
                nk = natk[1][slot]
                sp.dma_start(nk[:, 0:NT, :], kscr[1][0:SEQ, c].rearrange("(t p) n -> p t n", p=P)).then_inc(nat_qk[slot], 16)
                sp.dma_start(nk[0:TX, NT, :], kscr[1][SEQ:T, c]).then_inc(nat_qk[slot], 16)
                sp.dma_start(nk[:, 5:7, :], kscr[1][T:, c].rearrange("(t p) n -> p t n", p=P)).then_inc(nat_qk[slot], 16)

            def mla_q(j, slot):
                c = bass.ds(j * (2 * R_MLA), 2 * R_MLA)
                nq = natq[1][slot]
                sp.dma_start(nq[:, 0:NT, :], qscr[1][0:SEQ, c].rearrange("(t p) n -> p t n", p=P)).then_inc(nat_qk[slot], 16)
                sp.dma_start(nq[0:TX, NT, :], qscr[1][SEQ:T, c]).then_inc(nat_qk[slot], 16)

            for i in range(4):
                sp.wait_ge(st_out[i], stored(i, 30))
            sp.wait_ge(cka_out, 16)
            fox_qk(0, 0)
            fox_v(0)
            fox_qk(1, 1)
            with sp.Fori(0, PAIRS // 2 - 1) as i:
                for k in range(2):
                    sp.wait_ge(v_split, i * 2 + (k + 1))
                    fox_v(2 * i + (k + 1))
                    sp.wait_ge(g_ps, i * 36 + (18 * k + 6))
                    fox_qk(2 * i + (k + 2), k)
                sp.nop()
            sp.wait_ge(v_split, PAIRS - 1)
            fox_v(PAIRS - 1)

            def mlp_loads(layer, j0):
                def mload(j, src_of_up, c, n=0):
                    up, down = mlp_views(raw, j)
                    sp.wait_ge(lo_done, (j - 3) + 4 * n)
                    if src_of_up:
                        sp.dma_start(up, up_src(layer, c)).then_inc(raw_in[j % 4], 16)
                    else:
                        sp.dma_start(down, down_src(layer, c)).then_inc(raw_in[j % 4], 16)
                mload(j0, True, 0)
                with sp.Fori(0, NCH // 2 - 1) as i:
                    mload(j0 + 1, True, 2 * i + 1, i)
                    mload(j0 + 2, False, 2 * i, i)
                    mload(j0 + 3, True, 2 * i + 2, i)
                    mload(j0 + 4, False, 2 * i + 1, i)
                    sp.nop()
                mload(j0 + 29, True, NCH - 1)
                mload(j0 + 30, False, NCH - 2)
                mload(j0 + 31, False, NCH - 1)

            mlp_loads(0, MLP_A0)

            for j in range(KVD0, QU0):
                load(j)
            sp.wait_ge(x_ready, 24)
            sp.dma_start(zc[:, 5:7, :], io["cache_ckv"].rearrange("(t p) n -> p t n", p=P)).then_inc(lat_in, 16)
            sp.dma_start(gckv[:], io["ckv_norm"].partition_broadcast(P)).then_inc(lat_in, 16)
            sp.wait_ge(half_used, KVU0)
            sp.dma_start(krn[:, 5:7, :], io["cache_kr"].rearrange("(t p) n -> p t n", p=P)).then_inc(rope_in, 16)
            sp.dma_start(gq[:], io["q_norm"].partition_broadcast(P)).then_inc(rope_in, 16)
            for j in range(QU0, WO_B0):
                load(j)
            sp.wait_ge(z_norm, 5)
            ckp = io["o_ckv_p"]
            sp.dma_start(ckp[META:, :].rearrange("(t p) n -> p t n", p=P), zc[:, 0:NT, :]).then_inc(z_out, 16)
            sp.dma_start(io["o_ckv_s"], zc[0:SAM, NT, :]).then_inc(z_out, 16)
            sp.dma_start(ckp[0:META, :], zc[SAM:TX, NT, :]).then_inc(z_out, 16)
            sp.wait_ge(kr_ready, 1)
            krp = io["o_kr_p"]
            sp.dma_start(krp[META:, :].rearrange("(t p) n -> p t n", p=P), krn[:, 0:NT, :]).then_inc(z_out, 16)
            sp.dma_start(io["o_kr_s"], krn[0:SAM, NT, :]).then_inc(z_out, 16)
            sp.dma_start(krp[0:META, :], krn[SAM:TX, NT, :]).then_inc(z_out, 16)
            for n in range(28):
                t, blk = (n % 14) // 2, 2 * (n // 14) + n % 2
                rows = P if t != NT else TX
                r0 = P * t if t <= NT else T + P * (t - 5)
                sp.wait_ge(lat_evac, n + 1)
                sp.dma_start(kscr[1][r0:r0 + rows, 512 * blk:512 * blk + 512],
                             stn[0:rows, n % 4, :]).then_inc(st_out[n % 4], 16)
            for i in range(4):
                sp.wait_ge(st_out[i], stored(i, 30) + 16 * 7)
            mla_kv(0, 0)
            for n in range(20):
                t, g = n % 5, n // 5
                sp.wait_ge(lat_rope, n + 1)
                sp.dma_start(qscr[1][P * t:P * t + TILE_ROWS[t], 384 * g:384 * g + 384],
                             stn[0:TILE_ROWS[t], n % 4, 0:384]).then_inc(st_out[n % 4], 16)
            for i in range(4):
                sp.wait_ge(st_out[i], stored(i, 30) + 16 * 12)
            sp.wait_ge(z_out, 96)
            mla_q(0, 0)
            sp.wait_ge(kr_ps, 1)
            mla_kv(1, 1)
            mla_q(1, 1)
            for j in range(WO_B0, MLP_B0):
                load(j)
            with sp.Fori(0, PAIRS // 2 - 1) as i:
                for k in range(2):
                    sp.wait_ge(g_ps, i * 36 + (18 * k + 6 + 9 * HEADS))
                    mla_q(2 * i + (k + 2), k)
                    sp.wait_ge(v_split, i * 2 + (k + 1 + PAIRS))
                    mla_kv(2 * i + (k + 2), k)
                sp.nop()
            mlp_loads(1, MLP_B0)
            for t in range(5):
                sp.wait_ge(y_evac, t + 1)
                if t < NT:
                    sp.dma_start(io["y_p"][P * t:P * t + P, :], yst[:, t % 2, :]).then_inc(y_outs[t % 2], 16)
                else:
                    sp.dma_start(io["y_s"], yst[0:SAM, t % 2, :]).then_inc(y_outs[t % 2], 16)
            sp.wait_ge(y_outs[0], 48)
            sp.wait_ge(y_outs[1], 32)
            sp.wait_ge(z_out, 96)
            sp.wait_ge(lg_out, 48)

        @block.gpsimd
        def _(pool):
            g = nc.gpsimd
            g.memset(mhalf[:], -0.5).then_inc(setup_ready, 1)
            g.memset(sacc[:, T:5 * P], 1.0).then_inc(setup_ready, 1)
            g.memset(ss[:], 1.0).then_inc(setup_ready, 1)

            def add_squares(b, k):
                pool.wait_ge(sq_ready, KD * b + k + 1)
                if k > 1:
                    pool.wait_ge(sacc_ready, 7 * b + k - 1)
                g.tensor_tensor(sacc[:, 0:T], sacc[:, 0:T], sq[:, k % 2, :], ALU.add).then_inc(sacc_ready, 1)

            def sum_squares(b):
                for k in range(1, KD):
                    add_squares(b, k)

            def rstd(n):
                pool.wait_ge(var_ready, n + 1)
                g.tensor_tensor(rst[:], v5[:], mhalf[:], ALU.pow).then_inc(rstd_ready, 1)

            pool.wait_ge(setup_ready, 3)
            sum_squares(0)
            rstd(0)
            pool.wait_ge(small_in, 64)
            g.tensor_copy(cka[:, :, :, 0:HD], ckn[:, :, :].rearrange("p t (h r) -> p t h r", r=HD)).then_inc(cka_ready, 1)
            pool.wait_ge(F_ready, 1)
            g.tensor_copy(cka[:, :, :, HD:R_FOX], FK[:, 5:7, :, :]).then_inc(cka_ready, 1)
            for n in range(10, 30):
                kind, hf = BLOCKS[n // 5]
                t = n % 5
                pool.wait_ge(st_out[n % 4], stored(n % 4, n - 3))
                tab = FK if kind == "k" else FQ
                g.tensor_copy(stg[:, n % 4, :].rearrange("p (h r) -> p h r", r=R_FOX)[0:TILE_ROWS[t], :, HD:R_FOX],
                              tab[0:TILE_ROWS[t], t, 8 * hf:8 * hf + 8, :]).then_inc(aug_done, 1)

            def split_v(layer, j, slot, turn, after_av=False):
                if layer == 0:
                    pool.wait_ge(nat_v, j * 64 + 64)
                else:
                    pool.wait_ge(nat_qk[slot], turn * 80 + (80 + 40 * PAIRS))
                if after_av:
                    pool.wait_ge(av_done, j * 2 + (HEADS * layer - 2))
                views = []
                for t0, t1, rows in ((NT, 5, TX), (0, NT, P), (5, 7, P)):
                    if layer == 0:
                        src = natv0[0:rows, t0:t1, :].rearrange("p t (h d) -> p t h d", h=2)
                    else:
                        src = natk[1][slot][0:rows, t0:t1, :].rearrange("p t (h d) -> p t h d", h=2)[:, :, :, HD:2 * HD]
                    views.append((src, slice(0, rows), slice(t0, t1)))
                src, r, t = views[0]
                g.tensor_tensor(vh[r, slot, NT, :].rearrange("p (h d) -> p h d", h=2), src.rearrange("p t h d -> p (t h) d"),
                                ones[r, :].rearrange("p (h d) -> p h d", h=2), ALU.mult).then_inc(v_hi, 1)
                for src, r, t in views[1:]:
                    g.tensor_copy(vh[r, slot, t, :].rearrange("p t (h d) -> p t h d", h=2), src).then_inc(v_hi, 1)
                pool.wait_ge(v_hi, j * 3 + 3 + 3 * PAIRS * layer)
                for n, (src, r, t) in enumerate(views):
                    i = g.tensor_tensor(vl[r, slot, t, :].rearrange("p t (h d) -> p t h d", h=2), src,
                                        vh[r, slot, t, :].bitcast(F32).rearrange("p t (h d) -> p t h d", h=2), ALU.subtract)
                i.then_inc(v_split, 1)

            split_v(0, 0, 0, 0)
            split_v(0, 1, 1, 0)
            with pool.Fori(0, PAIRS // 2 - 1) as i:
                split_v(0, 2 * i + 2, 0, i + 1, True)
                split_v(0, 2 * i + 3, 1, i + 1, True)

            def mlp_finish(layer):
                n = T if layer == 0 else T1
                pool.wait_ge(r2T_ready, (KD - 1) * (layer + 1))
                for m in range(KD):
                    pool.wait_ge(acc_done, ACC_N * (layer + 1) - KD + m + 1)
                    g.tensor_tensor(acc[:, m, 0:n], acc[:, m, 0:n], r2T[:, 0:n], ALU.mult).then_inc(acc_scaled, 1)

            sum_squares(1)
            mlp_finish(0)
            rstd(1)
            for i in range(2):
                pool.wait_ge(zv_ready, i + 1)
                g.tensor_tensor(rc[:, i, :], ss[:, i, :], mhalf[:], ALU.pow).then_inc(zr_ready, 1)
            split_v(1, 0, 0, 0)
            split_v(1, 1, 1, 0)
            with pool.Fori(0, PAIRS // 2 - 1) as i:
                split_v(1, 2 * i + 2, 0, i + 1, True)
                split_v(1, 2 * i + 3, 1, i + 1, True)
            sum_squares(3)
            mlp_finish(1)
            rstd(2)

        @block.scalar
        def _(act):
            s = nc.scalar

            def hi(j, n=0):
                act.wait_ge(raw_in[j % 4], 16 * (j // 4 + 1) + 16 * n)
                if j >= 4:
                    act.wait_ge(half_used, j - 3 + 4 * n)
                if piece_gain(j, 0) is None:
                    r, c = piece_shape(j)
                    s.activation(wh[:, j % 4, 0:r * c], raw[:, j % 4, 0:r * c], ACT.Copy).then_inc(hi_done, 1)
                else:
                    a, b = view(wh, j), view(raw, j)
                    for k in range(4):
                        i = s.activation(a[:, k, :], b[:, k, :], ACT.Copy, scale=piece_gain(j, k))
                    i.then_inc(hi_done, 1)

            def square(b, k):
                if k == 0 and b:
                    act.wait_ge(stat_ps, b)
                if k >= 1 and 7 * b + max(k - 2, 0) > 0:
                    act.wait_ge(sacc_ready, 7 * b + max(k - 2, 0))
                dst = sacc[:, 0:T] if k == 0 else sq[:, k % 2, :]
                s.activation(dst, xT[:, k, :], ACT.Square).then_inc(sq_ready, 1)

            def gain_hi(b, k, gain):
                act.wait_ge(x_ready, KD * b + k + 1)
                if gain is None:
                    s.activation(xgh[:, k, :], xT[:, k, :], ACT.Copy).then_inc(gh_ready, 1)
                elif b < 4:
                    s.activation(xgh[:, k, :], xT[:, k, :], ACT.Copy,
                                 scale=gT[:, gain + k:gain + k + 1]).then_inc(gh_ready, 1)
                else:
                    s.activation(yT[:, k, :], xT[:, k, 0:T1], ACT.Copy,
                                 scale=gT[:, gain + k:gain + k + 1]).then_inc(y_scaled, 1)

            def square_and_gain(b, gain, pieces=None):
                for k in range(KD):
                    gain_hi(b, k, gain)
                    square(b, k)
                    if pieces is not None and k in (2, 4, 6):
                        hi(pieces + k // 2 - 1)

            act.wait_ge(gT_ready, 1)
            act.wait_ge(setup_ready, 3)
            for k in range(KD):
                gain_hi(0, k, 0)
                if k in (3, 7):
                    hi(k // 4)
            for k in range(KD):
                square(0, k)
            hi(2)
            hi(3)
            act.wait_ge(small_in, 64)
            s.activation(wfh[:], wf[:], ACT.Copy).then_inc(wf_hi, 1)
            act.wait_ge(rstd_ready, 2)
            for b, (kind, hf) in enumerate(BLOCKS):
                for t in range(5):
                    n = 5 * b + t
                    r = TILE_ROWS[t]
                    wait_tile(act, b, t)
                    if n >= 4:
                        act.wait_ge(st_out[n % 4], stored(n % 4, n - 3))
                    src = ps[0:r, n % 4, :]
                    if kind == "v":
                        dst = stg[0:r, n % 4, 0:512]
                    else:
                        src = src.rearrange("p (h d) -> p h d", d=HD)
                        dst = stg[0:r, n % 4, :].rearrange("p (h d) -> p h d", d=R_FOX)[:, :, 0:HD]
                    sc = (rst8 if kind == "q" else rst)[0:r, t:t + 1]
                    s.activation(dst, src, ACT.Copy, scale=sc).then_inc(blk_evac, 1)
                    if b == 1 and t == 1:
                        act.wait_ge(f_chain, 3)
                        s.activation(ft[:, 2, :], ft[:, 1, :], ACT.Exp, scale=-1.0).then_inc(f_exp, 1)
                if b == 0:
                    act.wait_ge(fT_ps, 1)
                    act.wait_ge(sacc_ready, 7)
                    s.activation(halves(fT), ps[0:HEADS, 6:8, 0:TH], ACT.Copy).then_inc(fT_ready, 1)
                if b < 4:
                    hi(2 * b + 4)
                    hi(2 * b + 5)

            def attention(layer):
                U0, G0, H0 = 5 * HEADS * layer, 9 * HEADS * layer, HEADS * layer

                def exp(h, c, u):
                    n = unit_keys(u)[1]
                    rows = P if u < NT else TX
                    off = P_OFF[u] + (64 if u < NT else 0)
                    act.wait_ge(max_done, h * 5 + (U0 + u + 1))
                    src, form = logits(u)
                    s.activation(form(prob[0:rows, c, off:off + n]), src, ACT.Exp,
                                 bias=nmx[0:rows, u:u + 1], accum_out=sm[0:rows, u:u + 1]).then_inc(exp_done, 1)

                def group(h, q, what):
                    act.wait_ge(g_ps, group_at(h, q) + (G0 + 1))
                    copies = what(3 + q % 3, qh, kh, pth)
                    for dst, src in copies[:-1]:
                        s.activation(dst, src, ACT.Copy)
                    dst, src = copies[-1]
                    s.activation(dst, src, ACT.Copy).then_inc(g_hi, 1)

                def turned(h, k):
                    group(h, place(h, "p", k), p_group(*P_PARTS[k]))

                def qk(h, k, slot):
                    group(h, place(h, "q", k), prep_group(layer, k, slot))

                def out(head, p, pair):
                    act.wait_ge(av_done, head + (H0 + 1))
                    s.activation(oh[64 * p:64 * p + 64, pair, :], pf[64 * p:64 * p + 64, 3072:3072 + T],
                                 ACT.Copy).then_inc(o_hi, 1)

                def scale3(h, c):
                    act.wait_ge(recip_done, h * 5 + (U0 + 4))
                    s.activation(prob[:, c, P_OFF[3] + 64:P_OFF[4]], prob[:, c, P_OFF[3] + 64:P_OFF[4]], ACT.Copy,
                                 scale=rs[:, 3:4]).then_inc(p3_ready, 1)

                def step(h, c, pair, first=False, last=False):
                    for u in range(3):
                        if not first:
                            turned(h, u)
                        if u == 0 and not first:
                            scale3(h - 1, 1 - c)
                        if u == 2 and not (isinstance(h, int) and h < 2):
                            out(h - 2, c, pair - 1)
                        if not last:
                            qk(h, u, 1 - c)
                        exp(h, c, u)
                    if not first:
                        turned(h, 3)
                        turned(h, 4)
                    exp(h, c, 3)
                    if not first:
                        turned(h, 5)
                    exp(h, c, 4)

                for k in range(3):
                    qk(-1, k, 0)
                step(0, 0, 0, first=True)
                step(1, 1, 0)
                with act.Fori(1, PAIRS - 1) as i:
                    step(2 * i, 0, i)
                    step(2 * i + 1, 1, i)
                step(HEADS - 2, 0, PAIRS - 1)
                step(HEADS - 1, 1, PAIRS - 1, last=True)
                for k in range(6):
                    turned(HEADS, k)
                    if k == 0:
                        scale3(HEADS - 1, 1)
                    if k == 2:
                        out(HEADS - 2, 0, PAIRS - 1)
                out(HEADS - 1, 1, PAIRS - 1)

            attention(0)

            for q in range(4):
                hi(WO_A0 + q)
            square_and_gain(1, 8, MLP_A0)

            def mlp(layer, j0, tail):
                n = T if layer == 0 else T1
                cnt = 2 * NCH * layer

                def hidden(c, par_c, used):
                    for m in range(2):
                        v = two_banks(m, n)
                        if m == 0:
                            act.wait_ge(u_ps, c + 1 + NCH * layer)
                        else:
                            act.wait_ge(half_used, used)
                        s.activation(v, v, ACT.Relu).then_inc(u_relu, 1)
                        act.wait_ge(u_relu, c * 2 + m + 1 + cnt)
                        s.activation(v, v, ACT.Square).then_inc(u_sq, 1)
                        act.wait_ge(u_sq, c * 2 + m + 1 + cnt)
                        s.activation(halves(hh[:, par_c, m, 0:n]), v, ACT.Copy).then_inc(u_hi, 1)

                hidden(0, 0, j0 + 1)
                with act.Fori(0, NCH // 2 - 1) as i:
                    for q in range(2):
                        hi(j0 + 2 * q + 3, i)
                        hi(j0 + 2 * q + 4, i)
                        hidden(2 * i + q + 1, (q + 1) % 2, 4 * i + (j0 + 2 * q + 2))
                hi(j0 + 31)
                if tail:
                    hi(j0 + 32)
                hidden(NCH - 1, 1, j0 + 30)
                if tail:
                    hi(j0 + 33)
                    hi(j0 + 34)

            mlp(0, MLP_A0, True)
            for k in range(KD):
                gain_hi(2, k, None)
            for k in range(KD):
                square(2, k)
            hi(QD0 + 1)
            for t in range(5):
                act.wait_ge(z_evac, 2 * t + 1)
                act.wait_ge(sacc_ready, 21)
                if t >= 2:
                    act.wait_ge(z_sq, t - 1)
                s.activation(sq[0:TILE_ROWS[t], t % 2, 0:KVR], zc[0:TILE_ROWS[t], t, :], ACT.Square,
                             accum_out=ss[0:TILE_ROWS[t], 0, t:t + 1]).then_inc(z_sq, 1)
            hi(KVU0)
            hi(KVU0 + 1)
            for t in range(5):
                act.wait_ge(z_evac, 10 + t + 1)
                act.wait_ge(z_sq, 5 + t - 1)
                s.activation(sq[0:TILE_ROWS[t], t % 2, 0:QR], zq[0:TILE_ROWS[t], t, :], ACT.Square,
                             accum_out=ss[0:TILE_ROWS[t], 1, t:t + 1]).then_inc(z_sq, 1)
            for f in range(2):
                act.wait_ge(zT_ps, f + 1)
                s.activation(ckvTh[:, f, :], pf[:, 1024 * f:1024 * f + KEYS], ACT.Copy).then_inc(zT_hi, 1)
            hi(QU0)
            hi(QU0 + 1)
            for n in range(48):
                if n == 28:
                    act.wait_ge(z_out, 96)
                    for f in range(3):
                        act.wait_ge(zT_ps, f + 3)
                        c = 2048 + 1024 * (f % 2)
                        s.activation(cqTh[:, f, :], pf[:, c:c + T], ACT.Copy).then_inc(zT_hi, 1)
                wait_lat(act, n)
                if n >= 4:
                    act.wait_ge(st_out[n % 4], stored(n % 4, 30) + 16 * (n // 4))
                if n < 28:
                    t = (n % 14) // 2
                    r = TX if t == NT else P
                    s.activation(stn[0:r, n % 4, :], ps[0:r, n % 4, :], ACT.Copy).then_inc(lat_evac, 1)
                else:
                    r = TILE_ROWS[(n - 28) % 5]
                    s.activation(stn[0:r, n % 4, 0:384], ps[0:r, n % 4, 0:384], ACT.Copy,
                                 scale=MLA_SCALE).then_inc(lat_evac, 1)
                if n == 13:
                    hi(QU0 + 2)
                if n == 27:
                    hi(QU0 + 3)
            act.wait_ge(kr_ps, 1)
            for sl in range(2):
                s.activation(kh[HD:R_MLA, sl, 336:KEYS], pf[0:ROPE, 3072:3584], ACT.Copy)
                i = s.activation(kh[HD:R_MLA, sl, 0:336], pf[0:ROPE, 3584:3920], ACT.Copy)
            i.then_inc(kr_T, 1)
            attention(1)
            for q in range(4):
                hi(WO_B0 + q)
            square_and_gain(3, 32, MLP_B0)
            mlp(1, MLP_B0, False)
            square_and_gain(4, 40)
            for t in range(5):
                r = P if t < NT else SAM
                act.wait_ge(y_ps, t + 1)
                act.wait_ge(rstd_ready, 4)
                if t >= 2:
                    act.wait_ge(y_outs[t % 2], 16 * (t // 2))
                s.activation(yst[0:r, t % 2, :], pf[0:r, 1024 * (t % 2):1024 * (t % 2) + D], ACT.Copy,
                             scale=rst[0:r, t:t + 1]).then_inc(y_evac, 1)

        @block.vector
        def _(dve):
            v = nc.vector
            chained = [0]

            def link(i):
                chained[0] += 1
                i.then_inc(f_chain, 1)
                dve.wait_ge(f_chain, chained[0])

            def lo(j, n=0):
                dve.wait_ge(raw_in[j % 4], 16 * (j // 4 + 1) + 16 * n)
                dve.wait_ge(hi_done, j + 1 + 4 * n)
                if piece_gain(j, 0) is None:
                    r, c = piece_shape(j)
                    v.tensor_tensor(wl[:, j % 4, 0:r * c], raw[:, j % 4, 0:r * c],
                                    wh[:, j % 4, 0:r * c].bitcast(F32), ALU.subtract).then_inc(lo_done, 1)
                else:
                    a, b, w = view(wl, j), view(raw, j), view(wh, j)
                    for k in range(4):
                        i = v.scalar_tensor_tensor(a[:, k, :], b[:, k, :], piece_gain(j, k),
                                                   w[:, k, :].bitcast(F32), ALU.mult, ALU.subtract)
                    i.then_inc(lo_done, 1)

            def gain_lo(b, k, gain):
                dve.wait_ge(x_ready, KD * b + k + 1)
                dve.wait_ge(gh_ready, KD * b + k + 1)
                if gain is None:
                    v.tensor_tensor(xgl[:, k, :], xT[:, k, :], xgh[:, k, :].bitcast(F32),
                                    ALU.subtract).then_inc(gl_ready, 1)
                else:
                    v.scalar_tensor_tensor(xgl[:, k, :], xT[:, k, :], gT[:, gain + k:gain + k + 1],
                                           xgh[:, k, :].bitcast(F32), ALU.mult, ALU.subtract).then_inc(gl_ready, 1)

            def add_squares(b, k):
                dve.wait_ge(sq_ready, KD * b + k + 1)
                if k > 1:
                    dve.wait_ge(sacc_ready, 7 * b + k - 1)
                v.tensor_tensor(sacc[:, 0:T], sacc[:, 0:T], sq[:, k % 2, :], ALU.add).then_inc(sacc_ready, 1)

            def variance(b, bank):
                dve.wait_ge(stat_ps, b + 1)
                v.tensor_scalar(v5[:], ps[:, bank, 0:5], 1.0 / D, EPS, ALU.mult, ALU.add).then_inc(var_ready, 1)

            dve.wait_ge(mask_in, 16)
            v.tensor_copy(mask[:], mraw[:]).then_inc(masks_ready, 1)
            dve.wait_ge(cst_in, 16)
            v.tensor_copy(idr[:], ident).then_inc(masks_ready, 1)
            dve.wait_ge(gT_ps, 1)
            v.tensor_copy(gT[:], ps[:, 6, 0:48]).then_inc(gT_ready, 1)
            for k in range(KD + 1):
                if k < KD:
                    dve.wait_ge(xT_ps, k + 1)
                    c = 1024 * (k % 4)
                    v.tensor_copy(xT[:, k, :], pf[:, c:c + T]).then_inc(x_ready, 1)
                if k >= 1:
                    gain_lo(0, k - 1, 0)
                if k in (4, 8):
                    lo(k // 4 - 1)
            variance(0, 6)
            dve.wait_ge(rstd_ready, 1)
            v.tensor_scalar(rst8[:], rst[:], FOX_SCALE, None, ALU.mult).then_inc(rstd_ready, 1)
            lo(2)
            lo(3)
            dve.wait_ge(wf_hi, 1)
            v.tensor_tensor(wfl[:], wf[:], wfh[:].bitcast(F32), ALU.subtract).then_inc(wf_lo, 1)

            dve.wait_ge(small_in, 64)
            dve.wait_ge(f_ps, 1)
            z = lg[:, 0:5, :].rearrange("p t h -> p (t h)")
            link(v.memset(lg[:, 0:5, :], 0.0))
            for t in range(5):
                r = TILE_ROWS[t]
                i = v.scalar_tensor_tensor(lg[0:r, t, :], ps[0:r, 4, 16 * t:16 * t + 16], rst[0:r, t:t + 1],
                                           bfb[0:r, :], ALU.mult, ALU.add)
            link(i)
            link(v.scalar_tensor_tensor(ft[:, 1, :], z, -1.0, z, ALU.mult, ALU.max))
            dve.wait_ge(f_exp, 1)
            link(v.tensor_scalar(ft[:, 3, :], ft[:, 2, :], 2.0, None, ALU.add))
            link(v.reciprocal(ft[:, 4, :], ft[:, 3, :]))
            link(v.tensor_tensor(ft[:, 0, :], ft[:, 2, :], ft[:, 4, :], ALU.mult))
            link(v.tensor_tensor(ft[:, 3, :], ft[:, 0, :], ft[:, 0, :], ALU.mult))
            link(v.tensor_scalar(ft[:, 4, :], ft[:, 3, :], 1.0 / 17, None, ALU.mult))
            for c in (15, 13, 11, 9, 7, 5, 3):
                link(v.scalar_tensor_tensor(ft[:, 4, :], ft[:, 4, :], 1.0 / c, ft[:, 3, :], ALU.add, ALU.mult))
            link(v.scalar_tensor_tensor(ft[:, 5, :], ft[:, 4, :], 1.0, ft[:, 0, :], ALU.add, ALU.mult))
            link(v.tensor_scalar(ft[:, 1, :], z, 0.0, None, ALU.min))
            link(v.scalar_tensor_tensor(z, ft[:, 5, :], -2.0, ft[:, 1, :], ALU.mult, ALU.add))
            assert chained[0] == F_CHAIN
            link(v.memset(FQ[:], 1.0))
            link(v.memset(FK[:], 1.0))
            lo(4)
            lo(5)
            dve.wait_ge(F_ps, 1)
            fp = ps[:, 5, 0:112].rearrange("p (t h) -> p t h", h=HEADS)
            for t, r in ((slice(0, NT), P), (slice(NT, 5), TX)):
                v.tensor_copy(FQ[0:r, t, :, 1], fp[0:r, t, :])
                v.tensor_scalar(FK[0:r, t, :, 0], fp[0:r, t, :], -1.0, None, ALU.mult)
            v.tensor_scalar(FK[:, 5:7, :, 0], fp[:, 5:7, :], -1.0, None, ALU.mult).then_inc(F_ready, 1)
            for j in range(6, 12):
                lo(j)

            def attention(layer):
                U0, G0, H0 = 5 * HEADS * layer, 9 * HEADS * layer, HEADS * layer

                def row_max(h, u):
                    n = unit_keys(u)[1]
                    rows = P if u < NT else TX
                    dve.wait_ge(s_ps, h * 5 + (U0 + u + 1))
                    v.tensor_reduce(nmx[0:rows, u:u + 1], logits(u)[0], AX.XY if u == NT - 1 else AX.X, ALU.max,
                                    negate=True).then_inc(max_done, 1)

                def recip(h, u):
                    rows = P if u < NT else TX
                    dve.wait_ge(exp_done, h * 5 + (U0 + u + 1))
                    v.reciprocal(rs[0:rows, u:u + 1], sm[0:rows, u:u + 1]).then_inc(recip_done, 1)

                def scale(h, c, u):
                    n = unit_keys(u)[1]
                    rows = P if u < NT else TX
                    off = P_OFF[u] + (64 if u < NT else 0)
                    dve.wait_ge(recip_done, h * 5 + (U0 + u + 1))
                    v.tensor_scalar(prob[0:rows, c, off:off + n], prob[0:rows, c, off:off + n], rs[0:rows, u:u + 1],
                                    None, ALU.mult).then_inc(p_ready, 1)

                def group(h, q, what):
                    bank = 3 + q % 3
                    dve.wait_ge(g_hi, group_at(h, q) + (G0 + 1))
                    both = list(zip(what(bank, ql, kl, ptl), what(bank, qh, kh, pth)))
                    for (dst, src), (hi_part, _) in both[:-1]:
                        v.tensor_tensor(dst, src, hi_part.bitcast(F32), ALU.subtract)
                    (dst, src), (hi_part, _) = both[-1]
                    v.tensor_tensor(dst, src, hi_part.bitcast(F32), ALU.subtract).then_inc(g_lo, 1)

                def turned(h, k):
                    group(h, place(h, "p", k), p_group(*P_PARTS[k]))

                def qk(h, k, slot):
                    group(h, place(h, "q", k), prep_group(layer, k, slot))

                def out(head, p, pair):
                    rows = slice(64 * p, 64 * p + 64)
                    dve.wait_ge(o_hi, head + (H0 + 1))
                    v.tensor_tensor(ol[rows, pair, :], pf[rows, 3072:3072 + T], oh[rows, pair, :].bitcast(F32),
                                    ALU.subtract).then_inc(o_lo, 1)

                def step(h, c, pair, first=False, last=False):
                    if not first:
                        turned(h, 0)
                    row_max(h, 0)
                    if not first:
                        recip(h - 1, 4)
                    if not last:
                        qk(h, 0, 1 - c)
                    if not first:
                        scale(h - 1, 1 - c, 4)
                        turned(h, 1)
                    row_max(h, 1)
                    recip(h, 0)
                    if not last:
                        qk(h, 1, 1 - c)
                    scale(h, c, 0)
                    if not first:
                        turned(h, 2)
                    row_max(h, 2)
                    if not (isinstance(h, int) and h < 2):
                        out(h - 2, c, pair - 1)
                    recip(h, 1)
                    if not last:
                        qk(h, 2, 1 - c)
                    row_max(h, 3)
                    scale(h, c, 1)
                    if not first:
                        turned(h, 3)
                    row_max(h, 4)
                    if not first:
                        turned(h, 4)
                    recip(h, 2)
                    if not first:
                        turned(h, 5)
                    scale(h, c, 2)
                    recip(h, 3)

                dve.wait_ge(half_used, WO_A0 if layer == 0 else WO_B0)
                for u in range(NT):
                    v.memset(prob[:, :, P_OFF[u]:P_OFF[u] + 64], 0.0)
                v.memset(prob[:, :, P_OFF[NT] + 336:P_OFF[NT] + 384], 0.0).then_inc(p_zero, 1)
                if layer == 1:
                    dve.wait_ge(kr_T, 1)
                    for sl in range(2):
                        v.tensor_tensor(kl[HD:R_MLA, sl, 336:KEYS], pf[0:ROPE, 3072:3584],
                                        kh[HD:R_MLA, sl, 336:KEYS].bitcast(F32), ALU.subtract)
                        i = v.tensor_tensor(kl[HD:R_MLA, sl, 0:336], pf[0:ROPE, 3584:3920],
                                            kh[HD:R_MLA, sl, 0:336].bitcast(F32), ALU.subtract)
                    i.then_inc(kr_lo, 1)
                for k in range(3):
                    qk(-1, k, 0)
                step(0, 0, 0, first=True)
                step(1, 1, 0)
                with dve.Fori(1, PAIRS - 1) as i:
                    step(2 * i, 0, i)
                    step(2 * i + 1, 1, i)
                step(HEADS - 2, 0, PAIRS - 1)
                step(HEADS - 1, 1, PAIRS - 1, last=True)
                turned(HEADS, 0)
                recip(HEADS - 1, 4)
                scale(HEADS - 1, 1, 4)
                for k in range(1, 6):
                    turned(HEADS, k)
                    if k == 2:
                        out(HEADS - 2, 0, PAIRS - 1)
                out(HEADS - 1, 1, PAIRS - 1)

            def residual_and_gain(b, j0, gain, n):
                for m in range(KD + 1):
                    if m < KD:
                        if m % 2:
                            dve.wait_ge(half_used, j0 + m // 2 + 1)
                        else:
                            dve.wait_ge(wo_ps, 4 * (b // 2) + m // 2 + 1)
                        a = halves(xT[:, m, 0:n])
                        v.tensor_tensor(a, a, two_banks(m % 2, n), ALU.add).then_inc(x_ready, 1)
                    if m in (2, 4, 6):
                        lo(j0 + 4 + m // 2 - 1)
                    if m >= 1:
                        gain_lo(b, m - 1, gain)

            def mlp(layer, j0, gain, tail):
                n = T if layer == 0 else T1
                b = 2 * layer + 2

                def hidden(c, par_c, m):
                    dve.wait_ge(u_hi, c * 2 + (m + 1 + 2 * NCH * layer))
                    v.tensor_tensor(halves(hl[:, par_c, m, 0:n]), two_banks(m, n),
                                    halves(hh[:, par_c, m, 0:n].bitcast(F32)), ALU.subtract).then_inc(u_lo, 1)

                def add(c, m, used):
                    if m < KD - 1:
                        dve.wait_ge(d_ps, c * 7 + (m + 1 + 7 * NCH * layer))
                    else:
                        dve.wait_ge(half_used, used)
                    dve.wait_ge(acc_done, c * KD + (m + 1 + ACC_N * layer))
                    a = halves(acc[:, m, 0:n])
                    v.tensor_tensor(a, a, two_banks(2 + m % 2, n), ALU.add).then_inc(acc_done, 1)

                dve.wait_ge(half_used, j0)
                for m in range(KD):
                    v.memset(acc[:, m, :], 0.0).then_inc(acc_done, 1)
                hidden(0, 0, 0)
                hidden(0, 0, 1)
                dve.wait_ge(stat_ps, 2 * layer + 2)
                v.tensor_scalar(r2T[:], pf[:, 3072:3072 + T], 1.0 / D, EPS, ALU.mult, ALU.add).then_inc(x_d, 1)
                with dve.Fori(0, NCH // 2 - 1) as i:
                    for q in range(2):
                        lo(j0 + 2 * q + 3, i)
                        lo(j0 + 2 * q + 4, i)
                        hidden(2 * i + q + 1, (q + 1) % 2, 0)
                        add(2 * i + q, 0, 0)
                        hidden(2 * i + q + 1, (q + 1) % 2, 1)
                        for m in range(1, KD):
                            add(2 * i + q, m, 4 * i + (j0 + 2 * q + 3))
                lo(j0 + 31)
                if tail:
                    lo(j0 + 32)
                hidden(NCH - 1, 1, 0)
                add(NCH - 2, 0, 0)
                hidden(NCH - 1, 1, 1)
                dve.wait_ge(x_d, layer + 1)
                for m in range(1, KD):
                    add(NCH - 2, m, j0 + 31)
                    c = slice(T // KD * (m - 1), T // KD * m if m < KD - 1 else T)
                    v.reciprocal(r2T[:, c], r2T[:, c]).then_inc(r2T_ready, 1)
                if tail:
                    lo(j0 + 33)
                for m in range(KD + 3):
                    if m < KD:
                        add(NCH - 1, m, j0 + 32)
                    if 1 <= m <= KD:
                        dve.wait_ge(acc_scaled, KD * layer + m)
                        v.tensor_tensor(xT[:, m - 1, 0:n], xT[:, m - 1, 0:n], acc[:, m - 1, 0:n],
                                        ALU.add).then_inc(x_ready, 1)
                    if 3 <= m and layer == 0:
                        gain_lo(b, m - 3, gain)
                    if 3 <= m < KD + 2 and layer == 1:
                        add_squares(b, m - 2)
                if layer == 0:
                    for k in range(1, KD):
                        add_squares(b, k)

            attention(0)
            for q in range(4):
                lo(WO_A0 + q)
            residual_and_gain(1, WO_A0, 8, T)
            mlp(0, MLP_A0, None, True)
            lo(QD0)
            variance(2, 5)
            lo(QD0 + 1)
            link(v.memset(zr[:], 0.0))
            dve.wait_ge(rstd_ready, 3)
            for zi in range(10):
                t = zi % 5
                r = TILE_ROWS[t]
                bank = Z_BANK[zi % 3]
                if t < NT:
                    dve.wait_ge(z_ps, zi - zi // 5 + 1)
                else:
                    dve.wait_ge(half_used, QD0 if zi < 5 else KVU0)
                if zi < 5:
                    v.tensor_scalar(zc[0:r, t, :], ps[0:r, bank, 0:KVR], rst[0:r, t:t + 1], None,
                                    ALU.mult).then_inc(z_evac, 1)
                    v.tensor_scalar(zr[0:r, t, :], ps[0:r, bank, KVR:KVR + ROPE], rst[0:r, t:t + 1], None,
                                    ALU.mult).then_inc(z_evac, 1)
                else:
                    v.tensor_scalar(zq[0:r, t, :], ps[0:r, bank, 0:QR], rst[0:r, t:t + 1], None,
                                    ALU.mult).then_inc(z_evac, 1)
                if zi == 4:
                    dve.wait_ge(z_sq, 5)
                    v.tensor_scalar(ss[:, 0, :], ss[:, 0, :], 1.0 / KVR, EPS, ALU.mult, ALU.add).then_inc(zv_ready, 1)
                    dve.wait_ge(zr_ready, 1)
                    dve.wait_ge(lat_in, 32)
                    for tt in range(5):
                        rr = TILE_ROWS[tt]
                        v.scalar_tensor_tensor(zc[0:rr, tt, :], zc[0:rr, tt, :], rc[0:rr, 0, tt:tt + 1],
                                               gckv[0:rr, :], ALU.mult, ALU.mult).then_inc(z_norm, 1)
                    lo(KVU0)
            lo(KVU0 + 1)
            dve.wait_ge(z_sq, 10)
            v.tensor_scalar(ss[:, 1, :], ss[:, 1, :], 1.0 / QR, EPS, ALU.mult, ALU.add).then_inc(zv_ready, 1)
            for f in range(2):
                dve.wait_ge(zT_hi, f + 1)
                v.tensor_tensor(ckvTl[:, f, :], pf[:, 1024 * f:1024 * f + KEYS], ckvTh[:, f, :].bitcast(F32),
                                ALU.subtract).then_inc(zT_lo, 1)
            dve.wait_ge(zr_ready, 2)
            dve.wait_ge(rope_in, 32)
            for t in range(5):
                r = TILE_ROWS[t]
                v.scalar_tensor_tensor(zq[0:r, t, :], zq[0:r, t, :], rc[0:r, 1, t:t + 1], gq[0:r, :],
                                       ALU.mult, ALU.mult).then_inc(z_norm, 1)
            cos = cst[:, C_COS:C_COS + 80].rearrange("p (t c) -> p t c", c=16)
            sin = cst[:, C_SIN:C_SIN + 80].rearrange("p (t c) -> p t c", c=16)
            x1, x2 = zr[:, :, 0:16], zr[:, :, 16:32]
            for i, (a, b) in enumerate(((x1, cos), (x2, sin), (x2, cos), (x1, sin))):
                v.tensor_tensor(krt[:, i, :, :], a, b, ALU.mult).then_inc(kr_chain, 1)
            dve.wait_ge(kr_chain, 4)
            v.tensor_tensor(krn[:, 0:5, 0:16], krt[:, 0, :, :], krt[:, 1, :, :], ALU.subtract)
            v.tensor_tensor(krn[:, 0:5, 16:32], krt[:, 2, :, :], krt[:, 3, :, :], ALU.add).then_inc(kr_ready, 1)
            lo(QU0)
            lo(QU0 + 1)
            for f in range(3):
                dve.wait_ge(zT_hi, f + 3)
                c = 2048 + 1024 * (f % 2)
                v.tensor_tensor(cqTl[:, f, :], pf[:, c:c + T], cqTh[:, f, :].bitcast(F32),
                                ALU.subtract).then_inc(zT_lo, 1)
            lo(QU0 + 2)
            lo(QU0 + 3)
            for n in range(20):
                t = n % 5
                r = TILE_ROWS[t]
                heads = stn[0:r, (n + 28) % 4, 0:384].rearrange("p (h c) -> p h c", c=R_MLA)
                x1, x2 = heads[:, :, HD:HD + 16], heads[:, :, HD + 16:R_MLA]
                cos = cst[0:r, C_COS + 16 * t:C_COS + 16 * t + 16].unsqueeze(1).to_broadcast([r, 4, 16])
                sin = cst[0:r, C_SIN + 16 * t:C_SIN + 16 * t + 16].unsqueeze(1).to_broadcast([r, 4, 16])
                dve.wait_ge(lat_evac, 28 + n + 1)
                if n:
                    dve.wait_ge(lat_rope, n)
                for i, (a, b) in enumerate(((x1, cos), (x2, sin), (x2, cos), (x1, sin))):
                    v.tensor_tensor(rtmp[0:r, i, :, :], a, b, ALU.mult).then_inc(rope_mul, 1)
                dve.wait_ge(rope_mul, 4 * n + 4)
                v.tensor_tensor(x1, rtmp[0:r, 0, :, :], rtmp[0:r, 1, :, :], ALU.subtract)
                v.tensor_tensor(x2, rtmp[0:r, 2, :, :], rtmp[0:r, 3, :, :], ALU.add).then_inc(lat_rope, 1)
            attention(1)
            for q in range(4):
                lo(WO_B0 + q)
            residual_and_gain(3, WO_B0, 32, T1)
            mlp(1, MLP_B0, 40, False)
            variance(4, 6)

        @block.tensor
        def _(pe):
            te = nc.tensor

            def mm(out, a, b, start, stop):
                return te.matmul(out, a, b, start=start, stop=stop)

            def token_stats(b, bank):
                pe.wait_ge(sacc_ready, 7 * (b + 1))
                for t in range(5):
                    i = mm(ps[:, bank, t:t + 1], sacc[:, P * t:P * t + P], ones[:, 0:1], True, True)
                i.then_inc(stat_ps, 1)

            def spread_stats(b):
                pe.wait_ge(sacc_ready, 7 * (b + 1))
                mm(ps[:, 6, :], ones, sacc[:, 0:512], True, True)
                mm(ps[:, 7, 0:T - 512], ones, sacc[:, 512:T], True, True).then_inc(stat_ps, 1)

            def tokens_product(out, xs, ws, k_n, rows, cols, gates=None, mid=None):
                (ah, al), (bh, bl) = xs, ws
                for k in range(k_n):
                    if gates:
                        gates(k)
                    mm(out, ah(k), bh(k), k == 0, False)
                    mm(out, ah(k), bl(k), False, False)
                    i = mm(out, al(k), bh(k), False, k == k_n - 1)
                    if mid and k == mid[0]:
                        i.then_inc(mid[1], 1)
                return i

            def x_tile(t):
                c = slice(P * t, P * t + TILE_ROWS[t])
                return (lambda k: xgh[:, k, c]), (lambda k: xgl[:, k, c])

            def split_halves(tensor, j, cols):
                return lambda k: view(tensor, j + k // 4)[:, k % 4, cols]

            pe.wait_ge(cst_in, 16)
            pe.wait_ge(gain_in, 96)
            te.transpose(ps[:, 6, 0:48], gn[:], ident[0:48, 0:48]).then_inc(gT_ps, 1)
            pe.wait_ge(x_in, 96)
            for k in range(KD):
                if k == 3:
                    pe.wait_ge(gT_ready, 1)
                if k >= 4:
                    pe.wait_ge(x_ready, k - 3)
                for t in range(5):
                    r = TILE_ROWS[t]
                    c = 1024 * (k % 4) + P * t
                    i = te.transpose(pf[:, c:c + r], xn[0:r, t, P * k:P * k + P], ident[0:r, 0:r])
                i.then_inc(xT_ps, 1)
            for b in range(6):
                for t in range(5):
                    n = 5 * b + t
                    if n >= 4:
                        pe.wait_ge(blk_evac, n - 3)
                    out = ps[0:TILE_ROWS[t], n % 4, :]

                    def gates(k):
                        if t == 0 and k % 4 == 0:
                            pe.wait_ge(lo_done, 2 * b + 1 + k // 4)
                        if n == 0:
                            pe.wait_ge(gl_ready, k + 1)
                    if n < 2:
                        pe.wait_ge(x_ready, 5 + 3 * n)
                    i = tokens_product(out, x_tile(t), (split_halves(wh, 2 * b, slice(0, 512)),
                                                        split_halves(wl, 2 * b, slice(0, 512))),
                                       KD, TILE_ROWS[t], 512, gates, (3, half_used) if t == NT else None)
                    i.then_inc(blk_ps if t < NT else half_used, 1)
                    if n == 1:
                        token_stats(0, 6)
                    if b == 1 and t == 0:
                        pe.wait_ge(fT_ready, 1)
                        for tt in range(5):
                            i = te.transpose(ps[0:TILE_ROWS[tt], 4, 16 * tt:16 * tt + 16],
                                             fT[:, P * tt:P * tt + TILE_ROWS[tt]], ident[0:HEADS, 0:HEADS])
                        i.then_inc(f_ps, 1)
                if b == 0:
                    pe.wait_ge(wf_lo, 1)
                    pe.wait_ge(var_ready, 1)
                    for k in range(KD):
                        for q, (w, x) in enumerate(((wfh, xgh), (wfh, xgl), (wfl, xgh))):
                            for half in range(2):
                                i = mm(ps[0:HEADS, 6 + half, 0:TH], w[:, k, :], x[:, k, TH * half:TH * half + TH],
                                       k == 0 and q == 0, k == KD - 1 and q == 2)
                    i.then_inc(fT_ps, 1)
                if b == 1:
                    pe.wait_ge(f_chain, F_CHAIN)
                    pe.wait_ge(small_in, 64)
                    U, M4 = cst[:, C_U:C_U + P], cst[0:TX, C_META:C_META + P]
                    tri, sam = cst[0:TX, C_TRI:C_TRI + TX], cst[:, C_SAM:C_SAM + TX]
                    sums = [(t, P, [(M4, lg[0:TX, NT, :])] + [(ones, lg[:, i, :]) for i in range(t)] + [(U, lg[:, t, :])])
                            for t in range(NT)]
                    sums += [(NT, TX, [(sam, lg[:, 5, :]), (sam, lg[:, 6, :]), (tri, lg[0:TX, NT, :])]),
                             (5, P, [(U, lg[:, 5, :])]), (6, P, [(ones, lg[:, 5, :]), (U, lg[:, 6, :])])]
                    for t, r, terms in sums:
                        for n, (a, l) in enumerate(terms):
                            i = mm(ps[0:r, 5, 16 * t:16 * t + 16], a, l, n == 0, n == len(terms) - 1)
                    i.then_inc(F_ps, 1)

            def attention(layer):
                U0, G0, H0 = 5 * HEADS * layer, 9 * HEADS * layer, HEADS * layer
                R = R_FOX if layer == 0 else R_MLA
                m0 = MD * layer

                def scores(h, c, u):
                    k0, n = unit_keys(u)
                    rows = P if u < NT else TX
                    q0 = P * u
                    before = [-1, -1, 0, 2, 3][u] + U0
                    if not (isinstance(h, int) and h * 5 + before < 1):
                        pe.wait_ge(exp_done, h * 5 + before)
                    a_h, a_l = qh[0:R, c, q0:q0 + rows], ql[0:R, c, q0:q0 + rows]
                    mk0 = n - P if u < NT else 0
                    mcol = m0 if u < NT else m0 + P
                    parts = 2 if u == NT - 1 else 1
                    for part in range(parts):
                        bank = S_BANK[u] + part
                        c0, c1 = n // parts * part, n // parts * (part + 1)
                        out = ps[0:rows, bank, 0:c1 - c0]
                        kk = slice(k0 + c0, k0 + c1)
                        mm(out, a_h, kh[0:R, c, kk], True, False)
                        if c1 > mk0:
                            te.matmul(ps[0:rows, bank, max(mk0 - c0, 0):c1 - c0], idr[:, 0:rows],
                                      mask[:, mcol + max(c0 - mk0, 0):mcol + c1 - mk0], start=False, stop=False,
                                      skip_group_check=True)
                        mm(out, a_h, kl[0:R, c, kk], False, False)
                        i = mm(out, a_l, kh[0:R, c, kk], False, True)
                    i.then_inc(s_ps, 1)

                def free_bank(h, q):
                    if not (isinstance(h, int) and group_at(h, q) + G0 < 3):
                        pe.wait_ge(g_lo, group_at(h, q) + (G0 - 2))

                def p_turn(h, c, k):
                    u, part = P_PARTS[k]
                    q = place(h, "p", k)
                    free_bank(h, q)
                    if u == 3:
                        pe.wait_ge(p3_ready, h + H0)
                    else:
                        pe.wait_ge(p_ready, h * 4 + (4 * H0 + [-3, -2, -1, 0, 0][u]))
                    bank = 3 + q % 3
                    if u == NT:
                        o = P_OFF[NT]
                        for j in range(3):
                            i = te.transpose(ps[:, bank, TX * j:TX * j + TX], prob[0:TX, 1 - c, o + P * j:o + P * j + P],
                                             ident[0:TX, 0:TX])
                    else:
                        n = min(u + 2, 4) if part == 0 else 1
                        for j in range(n):
                            b = j if part == 0 else 4
                            o = P_OFF[u] + (0 if b == 0 else TX + P * (b - 1))
                            i = te.transpose(ps[:, bank, P * j:P * j + P], prob[:, 1 - c, o:o + P], ident)
                    i.then_inc(g_ps, 1)

                def prep(h, g, nxt_c, nat):
                    q = place(h, "q", g)
                    nq, nk = natq[layer][nat], natk[layer][nat]
                    rk = R_FOX if layer == 0 else 2 * HD
                    kc = nxt_c * R_FOX if layer == 0 else 2 * HD * nxt_c
                    qc = nxt_c * R
                    free_bank(h, q)
                    bank = 3 + q % 3
                    if g == 0:
                        for t in range(NT):
                            i = te.transpose(ps[0:R, bank, P * t:P * t + P], nq[:, t, qc:qc + R], ident)
                    elif g == 1:
                        for t in range(2):
                            te.transpose(ps[0:rk, bank, P * t:P * t + P], nk[:, 5 + t, kc:kc + rk], ident)
                        te.transpose(ps[0:rk, bank, 256:336], nk[0:TX, NT, kc:kc + rk], ident[0:TX, 0:TX])
                        i = te.transpose(ps[0:R, bank, 336:416], nq[0:TX, NT, qc:qc + R], ident[0:TX, 0:TX])
                    else:
                        for t in range(NT):
                            i = te.transpose(ps[0:rk, bank, P * t:P * t + P], nk[:, t, kc:kc + rk], ident)
                    i.then_inc(g_ps, 1)

                def weighted_v(head, part, groups, pair, vs):
                    pe.wait_ge(g_lo, groups)
                    if part == 0:
                        pe.wait_ge(v_split, pair + (PAIRS * layer + 1))
                        if not (isinstance(head, int) and head + H0 < 1):
                            pe.wait_ge(o_lo, head + H0)
                    if part < 3:
                        ptv_h = pth[:, 0:2560].rearrange("p (b q) -> p b q", q=512)
                        ptv_l = ptl[:, 0:2560].rearrange("p (b q) -> p b q", q=512)
                        for b in ((0, 2, 1), (0, 2), (3, 4, 1))[part]:
                            t, rows = (NT, TX) if b == 0 else (b - 1, P)
                            first_q = 0 if part == 0 else 256
                            q0, q1 = max(first_q, P * max(b - 1, 0)), first_q + 256
                            out = pf[:, 3072 + q0:3072 + q1]
                            pr_h, pr_l = ptv_h[0:rows, b, q0:q1], ptv_l[0:rows, b, q0:q1]
                            te.matmul(out, vh[0:rows, vs, t, :], pr_h, start=(b == 0), stop=False, skip_group_check=True)
                            te.matmul(out, vh[0:rows, vs, t, :], pr_l, start=False, stop=False, skip_group_check=True)
                            te.matmul(out, vl[0:rows, vs, t, :], pr_h, start=False, stop=(b == 1), skip_group_check=True)
                        return
                    for b, (t, rows) in enumerate(((5, P), (6, P), (NT, TX))):
                        out = ps[:, 7, 0:TX]
                        c0 = 2560 + TX * b
                        te.matmul(out, vh[0:rows, vs, t, :], pth[0:rows, c0:c0 + TX], start=(b == 0), stop=False)
                        te.matmul(out, vh[0:rows, vs, t, :], ptl[0:rows, c0:c0 + TX], start=False, stop=False)
                        i = te.matmul(out, vl[0:rows, vs, t, :], pth[0:rows, c0:c0 + TX], start=False, stop=(b == 2))
                    i.then_inc(av_done, 1)

                def rest(h, part, pair, vs):
                    groups = p_split(h - 1, 4 if part < 3 else 5) + G0
                    weighted_v(h - 2, part, groups, pair, vs)

                def step(h, c, pair, nat, turn=0, first=False, last=False):
                    second = not (isinstance(h, int) and h < 2)
                    for u in range(5):
                        if not first and u < 4:
                            p_turn(h, c, u)
                            if u == 3:
                                p_turn(h, c, 4)
                        if u == 0:
                            pe.wait_ge(g_lo, qk_split(h) + G0)
                        scores(h, c, u)
                        if u < 3 and not last:
                            if u == 0 and c == 1:
                                pe.wait_ge(nat_qk[1 - nat], turn * 80 + (80 + 40 * PAIRS * layer))
                            prep(h, u, 1 - c, 1 - nat if c else nat)
                        if second and u < 2:
                            for part in ((1, 2), (3,))[u]:
                                rest(h, part, pair - 1, 1 - nat)
                        if u == 4 and not first:
                            p_turn(h, c, 5)
                            weighted_v(h - 1, 0, p_split(h, 1) + G0, pair if c else pair - 1, nat if c else 1 - nat)

                if layer == 0:
                    pe.wait_ge(F_ready, 1)
                    pe.wait_ge(blk_evac, 30)
                else:
                    pe.wait_ge(lat_evac, 48)
                    pe.wait_ge(kr_lo, 1)
                pe.wait_ge(masks_ready, 2)
                pe.wait_ge(nat_qk[0], 80 + 40 * PAIRS * layer)
                for g in range(3):
                    prep(-1, g, 0, 0)
                step(0, 0, 0, 0, first=True)
                step(1, 1, 0, 0)
                with pe.Fori(0, PAIRS // 2 - 1) as i:
                    step(4 * i + 2, 0, 2 * i + 1, 1)
                    step(4 * i + 3, 1, 2 * i + 1, 1, i + 1)
                    step(4 * i + 4, 0, 2 * i + 2, 0)
                    step(4 * i + 5, 1, 2 * i + 2, 0, i + 1)
                step(HEADS - 2, 0, PAIRS - 1, 1)
                step(HEADS - 1, 1, PAIRS - 1, 1, last=True)
                for k in range(6):
                    p_turn(HEADS, 0, k)
                    if k < 3:
                        rest(HEADS, k + 1, PAIRS - 1, 1)
                    if k == 4:
                        weighted_v(HEADS - 1, 0, p_split(HEADS, 1) + G0, PAIRS - 1, 1)
                for part in (1, 2, 3):
                    weighted_v(HEADS - 1, part, p_split(HEADS, 4 if part < 3 else 5) + G0, PAIRS - 1, 1)

            def out_projection(layer, j0):
                n = T if layer == 0 else T1
                b = 2 * layer + 1
                pe.wait_ge(o_lo, HEADS * (layer + 1))
                pe.wait_ge(exp_done, 5 * HEADS * (layer + 1))
                for m in range(KD):
                    j = j0 + m // 2
                    pe.wait_ge(lo_done, j + 1)
                    if m >= 2:
                        pe.wait_ge(x_ready, KD * b + m - 1)
                    c = slice(P * (m % 2), P * (m % 2) + P)
                    i = transposed(m % 2, view(wh, j), view(wl, j), c, oh, ol, KD, n)
                    i.then_inc(half_used if m % 2 else wo_ps, 1)

            def transposed(pair, w_h, w_l, c, x_h, x_l, k_n, n, gate=None):
                for k in range(k_n):
                    if gate:
                        gate(k)
                    for p, (w, x) in enumerate(((w_h, x_h), (w_h, x_l), (w_l, x_h))):
                        for t in range(2):
                            i = mm(ps[:, 2 * pair + t, 0:n // 2], w[:, k, c], x[:, k, t * (n // 2):(t + 1) * (n // 2)],
                                   k == 0 and p == 0, k == k_n - 1 and p == 2)
                return i

            def mlp(layer, j0):
                n = T if layer == 0 else T1
                b = 2 * layer + 1

                def up(c, j, it=0, first=False):
                    for m in range(2):
                        if m == 0:
                            pe.wait_ge(lo_done, it * 4 + (j + 1))
                        if not first:
                            pe.wait_ge(u_lo, c * 2 + (m - 1 + 2 * NCH * layer))
                        cols = slice(P * m, P * m + P)
                        i = transposed(m, mlp_views(wh, j)[0], mlp_views(wl, j)[0], cols, xgh, xgl, KD, n,
                                       (lambda k: pe.wait_ge(gl_ready, KD * b + k + 1)) if first and m == 0 else None)
                        i.then_inc(half_used if m else u_ps, 1)

                def down(c, j, par_c, it=0):
                    pe.wait_ge(lo_done, it * 4 + (j + 1))
                    pe.wait_ge(u_lo, c * 2 + (2 + 2 * NCH * layer))
                    for m in range(KD):
                        pe.wait_ge(acc_done, c * KD + (m + 7 + ACC_N * layer))
                        cols = slice(P * m, P * m + P)
                        i = transposed(2 + m % 2, mlp_views(wh, j)[1], mlp_views(wl, j)[1], cols,
                                       hh[:, par_c], hl[:, par_c], 2, n)
                        i.then_inc(half_used if m == KD - 1 else d_ps, 1)

                pe.wait_ge(x_ready, KD * b + KD - 1)
                up(0, j0, first=True)
                up(1, j0 + 1)
                spread_stats(b)
                pe.wait_ge(x_d, layer + 1)
                with pe.Fori(0, NCH // 2 - 1) as i:
                    for q in range(2):
                        down(2 * i + q, j0 + 2 * q + 2, q, i)
                        up(2 * i + q + 2, j0 + 2 * q + 3, i)
                down(NCH - 2, j0 + 30, 0)
                down(NCH - 1, j0 + 31, 1)

            attention(0)
            out_projection(0, WO_A0)
            mlp(0, MLP_A0)

            pe.wait_ge(acc_done, ACC_N)
            for zi in range(10):
                if zi == 3:
                    token_stats(2, 5)
                t, r = zi % 5, TILE_ROWS[zi % 5]
                j, w = (KVD0, KVR + ROPE) if zi < 5 else (QD0, QR)
                if zi >= 3:
                    pe.wait_ge(z_evac, 2 * (zi - 2) if zi < 8 else zi + 3)

                def gates(k):
                    if t == 0 and k % 4 == 0:
                        pe.wait_ge(lo_done, j + 1 + k // 4)
                    if zi == 0:
                        pe.wait_ge(gl_ready, 2 * KD + k + 1)
                i = tokens_product(ps[0:r, Z_BANK[zi % 3], 0:w], x_tile(t),
                                   (split_halves(wh, j, slice(0, w)), split_halves(wl, j, slice(0, w))),
                                   KD, r, w, gates, (3, half_used) if t == NT else None)
                i.then_inc(z_ps if t < NT else half_used, 1)
            pe.wait_ge(z_norm, 5)
            pe.wait_ge(lat_in, 32)
            pe.wait_ge(rope_in, 32)
            for f in range(2):
                for t in range(7):
                    r = TX if t == NT else P
                    c = 1024 * f + (P * t if t <= NT else T + P * (t - 5))
                    i = te.transpose(pf[:, c:c + r], zc[0:r, t, P * f:P * f + P], ident[0:r, 0:r])
                i.then_inc(zT_ps, 1)
            pe.wait_ge(zT_lo, 2)
            for n in range(28):
                t, blk = (n % 14) // 2, n % 2
                r = TX if t == NT else P
                c0 = P * t if t <= NT else T + P * (t - 5)
                j = KVU0 + n // 14
                if n % 14 == 0:
                    pe.wait_ge(lo_done, j + 1)
                if n >= 4:
                    pe.wait_ge(lat_evac, n - 3)
                i = tokens_product(ps[0:r, n % 4, :], ((lambda k: ckvTh[:, k, c0:c0 + r]), (lambda k: ckvTl[:, k, c0:c0 + r])),
                                   ((lambda k: view(wh, j)[:, k, 512 * blk:512 * blk + 512]),
                                    (lambda k: view(wl, j)[:, k, 512 * blk:512 * blk + 512])), 2, r, 512)
                i.then_inc(half_used if n % 14 == 13 else lat_ps, 1)
            pe.wait_ge(z_norm, 10)
            pe.wait_ge(var_ready, 2)
            for f in range(3):
                if f == 2:
                    pe.wait_ge(zT_lo, 3)
                for t in range(5):
                    r = TILE_ROWS[t]
                    c = 2048 + 1024 * (f % 2) + P * t
                    i = te.transpose(pf[:, c:c + r], zq[0:r, t, P * f:P * f + P], ident[0:r, 0:r])
                i.then_inc(zT_ps, 1)
            pe.wait_ge(zT_lo, 5)
            for n in range(20):
                t, r = n % 5, TILE_ROWS[n % 5]
                j = QU0 + n // 5
                c = slice(P * t, P * t + r)
                if t == 0:
                    pe.wait_ge(lo_done, j + 1)
                pe.wait_ge(lat_evac, 28 + n - 3)
                i = tokens_product(ps[0:r, n % 4, 0:384], ((lambda k: cqTh[:, k, c]), (lambda k: cqTl[:, k, c])),
                                   ((lambda k: view(wh, j)[:, k, :]), (lambda k: view(wl, j)[:, k, :])), 3, r, 384)
                i.then_inc(half_used if t == NT else lat_ps, 1)
            pe.wait_ge(kr_ready, 1)
            for t in range(NT):
                te.transpose(pf[0:ROPE, 3072 + P * t:3072 + P * t + P], krn[:, t, :], ident)
            for t in range(2):
                te.transpose(pf[0:ROPE, 3584 + P * t:3584 + P * t + P], krn[:, 5 + t, :], ident)
            te.transpose(pf[0:ROPE, 3840:3920], krn[0:TX, NT, :], ident[0:TX, 0:TX]).then_inc(kr_ps, 1)

            attention(1)
            out_projection(1, WO_B0)
            mlp(1, MLP_B0)
            pe.wait_ge(y_scaled, KD)
            for t in range(5):
                r = P if t < NT else SAM
                if t >= 2:
                    pe.wait_ge(y_evac, t - 1)
                for k in range(KD):
                    c = 1024 * (t % 2) + P * k
                    i = te.transpose(pf[0:r, c:c + P], yT[:, k, P * t:P * t + r], ident)
                i.then_inc(y_ps, 1)
                if t == 1:
                    token_stats(4, 6)


def constants():
    import numpy as np
    c = np.zeros((P, C_N), np.float32)
    c[:, C_ID:C_ID + P] = np.eye(P)
    c[:, C_U:C_U + P] = np.triu(np.ones((P, P)))
    c[:, C_ONE:C_ONE + P] = 1
    c[SAM:TX, C_META:C_META + P] = 1
    c[0:SAM, C_TRI:C_TRI + SAM] = np.triu(np.ones((SAM, SAM)))
    c[SAM:TX, C_TRI + SAM:C_TRI + TX] = np.triu(np.ones((META, META)))
    c[:, C_SAM:C_SAM + SAM] = 1
    pos = np.zeros((5, P), np.float32)
    for t in range(NT):
        pos[t] = META + P * t + np.arange(P)
    pos[NT, 0:SAM] = PAST + np.arange(SAM)
    pos[NT, SAM:TX] = np.arange(META)
    half = ROPE // 2
    inv = (np.float32(1.0) / np.power(np.float32(10000.0), np.arange(half, dtype=np.float32) * np.float32(2.0 / ROPE))).astype(np.float32)
    ang = (pos[:, :, None] * inv[None, None, :]).astype(np.float32)
    c[:, C_COS:C_COS + 80] = np.cos(ang).transpose(1, 0, 2).reshape(P, 80)
    c[:, C_SIN:C_SIN + 80] = np.sin(ang).transpose(1, 0, 2).reshape(P, 80)
    NEG = -1e30
    m = np.zeros((P, M_N), np.float32)
    r = np.arange(P)
    for layer in range(2):
        d = m[:, MD * layer:MD * layer + P]
        d[:] = np.where(r[None, :] <= r[:, None], 0, NEG) if layer == 0 else np.where(r[None, :] // 64 <= r[:, None] // 64, 0, NEG)
        e = m[:, MD * layer + P:MD * layer + MD]
        rs, rm = np.arange(SAM), np.arange(META)
        e[0:SAM, PAST + SAM:] = NEG
        e[SAM:TX, 0:PAST + SAM] = NEG
        if layer == 0:
            e[0:SAM, PAST:PAST + SAM] = np.where(rs[None, :] <= rs[:, None], 0, NEG)
            e[SAM:TX, PAST + SAM:] = np.where(rm[None, :] <= rm[:, None], 0, NEG)
    return c, m


_INS = [("x_prompt", "x_prompt", (SEQ, D)), ("x_sample", "x_sample", (SAM, D)), ("meta_tokens", "meta_tokens", (META, D)),
        ("cache_k", "cache_fox_k", (PAST, D)), ("cache_v", "cache_fox_v", (PAST, D)),
        ("cache_logf", "cache_fox_logf", (PAST, HEADS)), ("cache_ckv", "cache_mla_ckv", (PAST, KVR)),
        ("cache_kr", "cache_mla_krope", (PAST, ROPE)), ("norm_mix", "norm_mix", (2, D)), ("norm_ffn", "norm_ffn", (2, D)),
        ("w_in_a", "w_in_a", (1, D, 3 * D + HEADS)), ("b_f", "b_f", (HEADS,)), ("w_o_a", "w_o_a", (1, D, D)),
        ("kv_norm", "kv_norm", (D,)), ("w_kv_down", "w_kv_down", (D, KVR + ROPE)), ("ckv_norm", "ckv_norm", (KVR,)),
        ("w_kv_up", "w_kv_up", (KVR, HEADS * 2 * HD)), ("w_q_down", "w_q_down", (1, D, QR)), ("q_norm", "q_norm", (QR,)),
        ("w_q_up", "w_q_up", (1, QR, HEADS * R_MLA)), ("w_o_b", "w_o_b", (1, D, D)), ("w_up", "w_up", (2, D, DFF)),
        ("w_down", "w_down", (2, DFF, D)), ("final_norm", "final_norm", (D,))]
_OUTS = [("y_p", (SEQ, D), (1, SEQ, D)), ("y_s", (SAM, D), (1, SAM, D)),
         ("o_k_p", (META + SEQ, D), (1, 1, META + SEQ, HEADS, HD)), ("o_v_p", (META + SEQ, D), (1, 1, META + SEQ, HEADS, HD)),
         ("o_lf_p", (META + SEQ, HEADS), (1, 1, META + SEQ, HEADS)), ("o_ckv_p", (META + SEQ, KVR), (1, META + SEQ, KVR)),
         ("o_kr_p", (META + SEQ, ROPE), (1, META + SEQ, ROPE)),
         ("o_k_s", (SAM, D), (1, 1, SAM, HEADS, HD)), ("o_v_s", (SAM, D), (1, 1, SAM, HEADS, HD)),
         ("o_lf_s", (SAM, HEADS), (1, 1, SAM, HEADS)), ("o_ckv_s", (SAM, KVR), (1, SAM, KVR)),
         ("o_kr_s", (SAM, ROPE), (1, SAM, ROPE))]


def kernel(**inputs):
    import numpy as np
    import concourse.bacc as bacc
    from concourse.bass_utils import run_bass_kernel_spmd

    nc = bacc.Bacc("TRN2", target_bir_lowering=False, num_devices=1)
    arrays, io = {}, {}
    for name, key, shape in _INS:
        a = np.ascontiguousarray(inputs[key]).reshape(shape)
        arrays[f"in_{name}"] = a
        io[name] = nc.dram_tensor(f"in_{name}", a.shape, mybir.dt.from_np(a.dtype), kind="ExternalInput").ap()
    for name, a in zip(("cst", "masks"), constants()):
        arrays[f"in_{name}"] = a
        io[name] = nc.dram_tensor(f"in_{name}", a.shape, F32, kind="ExternalInput").ap()
    for name, shape, _ in _OUTS:
        io[name] = nc.dram_tensor(f"out_{name}", shape, F32, kind="ExternalOutput").ap()
    build(nc, io)
    r = run_bass_kernel_spmd(nc, [arrays], core_ids=[0])
    return tuple(np.asarray(r.results[0][f"out_{name}"]).reshape(ret) for name, _, ret in _OUTS)
```
